# Optimizing a Trainium2 kernel written in Bass

```python
import jax, jax.numpy as jnp
from jax import lax
import numpy as np

D_MODEL = 2048
BATCH = 1
SEQ = 256
DEPTH = 1

GLA_HEADS = 4
GLA_DK = D_MODEL // 16
GLA_DV = D_MODEL // 8
GLA_GATE_RANK = 16
GLA_GATE_TAU = 16.0
GLA_CHUNK = 64
CONV_WIDTH = 4

NSA_HEADS = 8
NSA_KV_HEADS = 2
NSA_GROUP = NSA_HEADS // NSA_KV_HEADS
NSA_HEAD_DIM = 128
CMP_BLOCK = 32
CMP_STRIDE = 16
CMP_HIDDEN = 128
SEL_BLOCK = 64
SEL_TOPK = 16
WINDOW = 512
Q_BLOCK = 128

D_FF = -(-8 * D_MODEL // (3 * 256)) * 256
EPS = 1e-6
NEG = -1e30

GLA_QK = GLA_HEADS * GLA_DK
GLA_VW = GLA_HEADS * GLA_DV
GLA_QKV = 2 * GLA_QK + GLA_VW
NSA_QW = NSA_HEADS * NSA_HEAD_DIM
NSA_KVW = NSA_KV_HEADS * NSA_HEAD_DIM
MIX_WIDTH = GLA_VW + NSA_QW
PROJ_SIZES = (GLA_QKV, GLA_GATE_RANK, GLA_VW, NSA_QW, NSA_KVW, NSA_KVW, NSA_KVW, NSA_KVW, NSA_KVW, NSA_KVW, 3 * NSA_HEADS)
PROJ_WIDTH = sum(PROJ_SIZES)


def rms_norm(u, g):
    uf = u.astype(jnp.float32)
    y = uf * lax.rsqrt(jnp.mean(uf * uf, axis=-1, keepdims=True) + EPS)
    return (y * g.astype(jnp.float32)).astype(u.dtype)

def causal_short_conv(u, w):
    s = u.shape[1]
    up = jnp.pad(u, ((0, 0), (CONV_WIDTH - 1, 0), (0, 0)))
    return sum(up[:, i:i + s] * w[i] for i in range(CONV_WIDTH))

def gla_mixer(q, k, v, gate_lr, out_gate, gate_w2, gate_b, norm_g):
    b_, s, _ = q.shape
    h, c = GLA_HEADS, GLA_CHUNK
    n_chunks = s // c
    log_a = jax.nn.log_sigmoid((gate_lr @ gate_w2 + gate_b).astype(jnp.float32)) / GLA_GATE_TAU

    def chunks(u, d):
        return u.reshape(b_, n_chunks, c, h, d).transpose(1, 0, 3, 2, 4)

    qc = chunks(q.astype(jnp.float32) * GLA_DK ** -0.5, GLA_DK)
    kc = chunks(k.astype(jnp.float32), GLA_DK)
    vc = chunks(v.astype(jnp.float32), GLA_DV)
    gc = chunks(log_a, GLA_DK)
    causal = jnp.tril(jnp.ones((c, c), dtype=bool))[:, :, None]

    def step(state, inp):
        qi, ki, vi, gi = inp
        b = jnp.cumsum(gi, axis=2)
        o_inter = jnp.einsum('bhtd,bhde->bhte', qi * jnp.exp(b), state)
        decay = jnp.exp(jnp.where(causal, b[:, :, :, None, :] - b[:, :, None, :, :], -jnp.inf))
        scores = jnp.einsum('bhtd,bhsd,bhtsd->bhts', qi, ki, decay)
        o_intra = jnp.einsum('bhts,bhse->bhte', scores, vi)
        b_last = b[:, :, -1:, :]
        state = (jnp.exp(b_last[:, :, 0, :])[..., None] * state
                 + jnp.einsum('bhsd,bhse->bhde', ki * jnp.exp(b_last - b), vi))
        return state, o_inter + o_intra

    state0 = jnp.zeros((b_, h, GLA_DK, GLA_DV), jnp.float32)
    _, o = lax.scan(step, state0, (qc, kc, vc, gc))
    o = o.transpose(1, 0, 3, 2, 4).reshape(b_, s, h, GLA_DV)
    o = rms_norm(o, norm_g) * jax.nn.silu(out_gate.astype(jnp.float32)).reshape(b_, s, h, GLA_DV)
    return o.reshape(b_, s, GLA_VW).astype(q.dtype)

def nsa_mixer(q, kc_raw, vc_raw, ks_raw, vs_raw, kw_raw, vw_raw, gate_logits,
              q_g, kc_g, ks_g, kw_g, k_pos, k_w1, k_w2, v_pos, v_w1, v_w2):
    b_, s, _ = q.shape
    hk, g, dh = NSA_KV_HEADS, NSA_GROUP, NSA_HEAD_DIM
    n_cmp = (s - CMP_BLOCK) // CMP_STRIDE + 1
    n_sel_blocks = s // SEL_BLOCK
    n_sel = min(SEL_TOPK, n_sel_blocks)
    scale = dh ** -0.5

    def heads(u, n):
        return u.reshape(b_, s, n, dh).transpose(0, 2, 1, 3)

    qh = rms_norm(heads(q, NSA_HEADS), q_g).reshape(b_, hk, g, s, dh)

    cmp_idx = jnp.arange(n_cmp)[:, None] * CMP_STRIDE + jnp.arange(CMP_BLOCK)[None, :]

    def compress(u, pos, w1, w2):
        blocks = u[:, :, cmp_idx] + pos
        flat = blocks.reshape(b_, hk, n_cmp, CMP_BLOCK * dh)
        return jax.nn.silu(flat @ w1) @ w2

    k_cmp = rms_norm(compress(heads(kc_raw, hk), k_pos, k_w1, k_w2), kc_g)
    v_cmp = compress(heads(vc_raw, hk), v_pos, v_w1, v_w2)
    cmp_end = jnp.arange(n_cmp) * CMP_STRIDE + CMP_BLOCK - 1

    c_start = jnp.arange(n_cmp)[:, None] * CMP_STRIDE
    s_start = jnp.arange(n_sel_blocks)[None, :] * SEL_BLOCK
    overlap = jnp.clip(jnp.minimum(c_start + CMP_BLOCK, s_start + SEL_BLOCK)
                       - jnp.maximum(c_start, s_start), 0, None).astype(jnp.float32) / CMP_STRIDE

    k_sel = rms_norm(heads(ks_raw, hk), ks_g).reshape(b_, hk, n_sel_blocks, SEL_BLOCK, dh)
    v_sel = heads(vs_raw, hk).reshape(b_, hk, n_sel_blocks, SEL_BLOCK, dh)
    win_pad = ((0, 0), (0, 0), (WINDOW, 0), (0, 0))
    k_win = jnp.pad(rms_norm(heads(kw_raw, hk), kw_g), win_pad)
    v_win = jnp.pad(heads(vw_raw, hk), win_pad)
    gates = jax.nn.sigmoid(gate_logits.astype(jnp.float32)).reshape(b_, s, hk, g, 3).transpose(0, 2, 3, 1, 4)

    gather_blocks = jax.vmap(jax.vmap(lambda blk, ix: blk[ix]))
    sel_offsets = jnp.arange(SEL_BLOCK)
    win_offsets = jnp.arange(WINDOW + Q_BLOCK)
    sel_ids = jnp.arange(n_sel_blocks)

    def query_block(s0):
        t = s0 + jnp.arange(Q_BLOCK)
        qb = lax.dynamic_slice_in_dim(qh, s0, Q_BLOCK, axis=3)

        sc = jnp.einsum('bhgqd,bhnd->bhgqn', qb, k_cmp).astype(jnp.float32) * scale
        mc = cmp_end[None, :] <= t[:, None]
        pc = jax.nn.softmax(jnp.where(mc, sc, NEG), axis=-1) * mc
        o_cmp = jnp.einsum('bhgqn,bhnd->bhgqd', pc.astype(v_cmp.dtype), v_cmp)

        imp = jnp.einsum('bhgqn,nj->bhqj', pc, overlap)
        jt = (t // SEL_BLOCK)[:, None]
        forced = (sel_ids == 0) | (sel_ids == jt) | (sel_ids == jt - 1)
        imp = jnp.where(sel_ids > jt, -jnp.inf, jnp.where(forced, jnp.inf, imp))
        _, idx = lax.top_k(imp, n_sel)
        ks = gather_blocks(k_sel, idx).reshape(b_, hk, Q_BLOCK, n_sel * SEL_BLOCK, dh)
        vs = gather_blocks(v_sel, idx).reshape(b_, hk, Q_BLOCK, n_sel * SEL_BLOCK, dh)
        kpos = (idx[..., None] * SEL_BLOCK + sel_offsets).reshape(b_, hk, Q_BLOCK, n_sel * SEL_BLOCK)
        ms = (kpos <= t[:, None])[:, :, None]
        ss = jnp.einsum('bhgqd,bhqkd->bhgqk', qb, ks).astype(jnp.float32) * scale
        ps = jax.nn.softmax(jnp.where(ms, ss, NEG), axis=-1)
        o_sel = jnp.einsum('bhgqk,bhqkd->bhgqd', ps.astype(vs.dtype), vs)

        kwb = lax.dynamic_slice_in_dim(k_win, s0, WINDOW + Q_BLOCK, axis=2)
        vwb = lax.dynamic_slice_in_dim(v_win, s0, WINDOW + Q_BLOCK, axis=2)
        wpos = s0 - WINDOW + win_offsets
        dist = t[:, None] - wpos[None, :]
        mw = (wpos[None, :] >= 0) & (dist >= 0) & (dist < WINDOW)
        sw = jnp.einsum('bhgqd,bhkd->bhgqk', qb, kwb).astype(jnp.float32) * scale
        pw = jax.nn.softmax(jnp.where(mw, sw, NEG), axis=-1)
        o_win = jnp.einsum('bhgqk,bhkd->bhgqd', pw.astype(vwb.dtype), vwb)

        gb = lax.dynamic_slice_in_dim(gates, s0, Q_BLOCK, axis=3)
        return gb[..., 0:1] * o_cmp + gb[..., 1:2] * o_sel + gb[..., 2:3] * o_win

    n_blocks = s // Q_BLOCK
    out = lax.map(query_block, jnp.arange(n_blocks) * Q_BLOCK)
    out = out.transpose(1, 0, 4, 2, 3, 5).reshape(b_, s, NSA_QW)
    return out.astype(q.dtype)

def hybrid_layer(x, attn_norm_g, w_in, gla_conv_w, gla_gate_w2, gla_gate_b, gla_norm_g,
                 nsa_q_norm_g, nsa_kc_norm_g, nsa_ks_norm_g, nsa_kw_norm_g,
                 cmp_k_pos, cmp_k_w1, cmp_k_w2, cmp_v_pos, cmp_v_w1, cmp_v_w2,
                 w_out, ffn_norm_g, w_gate, w_up, w_down):
    n = rms_norm(x, attn_norm_g)
    proj = n @ w_in
    offsets = np.cumsum(PROJ_SIZES)[:-1].tolist()
    (g_qkv, g_lr, g_out, nq, kc, vc, ks, vs, kw, vw, ng) = jnp.split(proj, offsets, axis=-1)
    g_qkv = jax.nn.silu(causal_short_conv(g_qkv, gla_conv_w))
    gq, gk, gv = jnp.split(g_qkv, [GLA_QK, 2 * GLA_QK], axis=-1)
    gla_out = gla_mixer(gq, gk, gv, g_lr, g_out, gla_gate_w2, gla_gate_b, gla_norm_g)
    nsa_out = nsa_mixer(nq, kc, vc, ks, vs, kw, vw, ng,
                        nsa_q_norm_g, nsa_kc_norm_g, nsa_ks_norm_g, nsa_kw_norm_g,
                        cmp_k_pos, cmp_k_w1, cmp_k_w2, cmp_v_pos, cmp_v_w1, cmp_v_w2)
    h = x + jnp.concatenate([gla_out, nsa_out], axis=-1) @ w_out
    m = rms_norm(h, ffn_norm_g)
    return h + (jax.nn.silu(m @ w_gate) * (m @ w_up)) @ w_down

def first_inputs(seed: int = 0) -> dict:
    key = jax.random.key(seed)
    ks = jax.random.split(key, 22)

    def dense(k, shape, fan_in):
        return jax.random.normal(k, shape, jnp.float32) * fan_in ** -0.5

    def gain(k, d):
        return 1.0 + 0.02 * jax.random.normal(k, (DEPTH, d), jnp.float32)

    dh = NSA_HEAD_DIM
    return {
        'x': jax.random.normal(ks[0], (BATCH, SEQ, D_MODEL), jnp.float32),
        'attn_norm_g': gain(ks[1], D_MODEL),
        'w_in': dense(ks[2], (DEPTH, D_MODEL, PROJ_WIDTH), D_MODEL),
        'gla_conv_w': dense(ks[3], (DEPTH, CONV_WIDTH, GLA_QKV), CONV_WIDTH),
        'gla_gate_w2': dense(ks[4], (DEPTH, GLA_GATE_RANK, GLA_QK), GLA_GATE_RANK),
        'gla_gate_b': 0.02 * jax.random.normal(ks[5], (DEPTH, GLA_QK), jnp.float32),
        'gla_norm_g': gain(ks[6], GLA_DV),
        'nsa_q_norm_g': gain(ks[7], dh),
        'nsa_kc_norm_g': gain(ks[8], dh),
        'nsa_ks_norm_g': gain(ks[9], dh),
        'nsa_kw_norm_g': gain(ks[10], dh),
        'cmp_k_pos': 0.1 * jax.random.normal(ks[11], (DEPTH, CMP_BLOCK, dh), jnp.float32),
        'cmp_k_w1': dense(ks[12], (DEPTH, CMP_BLOCK * dh, CMP_HIDDEN), CMP_BLOCK * dh),
        'cmp_k_w2': dense(ks[13], (DEPTH, CMP_HIDDEN, dh), CMP_HIDDEN),
        'cmp_v_pos': 0.1 * jax.random.normal(ks[14], (DEPTH, CMP_BLOCK, dh), jnp.float32),
        'cmp_v_w1': dense(ks[15], (DEPTH, CMP_BLOCK * dh, CMP_HIDDEN), CMP_BLOCK * dh),
        'cmp_v_w2': dense(ks[16], (DEPTH, CMP_HIDDEN, dh), CMP_HIDDEN),
        'w_out': dense(ks[17], (DEPTH, MIX_WIDTH, D_MODEL), MIX_WIDTH),
        'ffn_norm_g': gain(ks[18], D_MODEL),
        'w_gate': dense(ks[19], (DEPTH, D_MODEL, D_FF), D_MODEL),
        'w_up': dense(ks[20], (DEPTH, D_MODEL, D_FF), D_MODEL),
        'w_down': dense(ks[21], (DEPTH, D_FF, D_MODEL), D_FF),
    }

def first_block(x, attn_norm_g, w_in, gla_conv_w, gla_gate_w2, gla_gate_b, gla_norm_g,
              nsa_q_norm_g, nsa_kc_norm_g, nsa_ks_norm_g, nsa_kw_norm_g,
              cmp_k_pos, cmp_k_w1, cmp_k_w2, cmp_v_pos, cmp_v_w1, cmp_v_w2,
              w_out, ffn_norm_g, w_gate, w_up, w_down):
    for l in range(DEPTH):
        x = hybrid_layer(x, attn_norm_g[l], w_in[l], gla_conv_w[l], gla_gate_w2[l], gla_gate_b[l],
                         gla_norm_g[l], nsa_q_norm_g[l], nsa_kc_norm_g[l], nsa_ks_norm_g[l],
                         nsa_kw_norm_g[l], cmp_k_pos[l], cmp_k_w1[l], cmp_k_w2[l], cmp_v_pos[l],
                         cmp_v_w1[l], cmp_v_w2[l], w_out[l], ffn_norm_g[l], w_gate[l], w_up[l],
                         w_down[l])
    return x


DEPTH_2 = 2

GRID_W = 64
CTX_LEN = 256
HEAD_DIM = 128
HALF_DIM = HEAD_DIM // 2
AXIS_FREQS = HEAD_DIM // 4
ROPE_THETA = 10000.0
N_HEADS_A = 8
N_KV_A = 2
N_HEADS_B = 8
N_KV_B = 2
G_A = N_HEADS_A // N_KV_A
G_B = N_HEADS_B // N_KV_B
WINDOW_2 = 128
BAND = Q_BLOCK + 2 * WINDOW_2
ATTN_SCALE = HEAD_DIM ** -0.5
NEG_INF = -1e30
Q_W = (N_HEADS_A + N_HEADS_B) * HEAD_DIM
KV_A_W = N_KV_A * HEAD_DIM
KV_B_W = N_KV_B * HEAD_DIM
KV_W = 2 * KV_A_W + 2 * KV_B_W
ATTN_WIDTH = Q_W
EVEN_IN = Q_W + KV_W + ATTN_WIDTH
POOL_WIDTH = D_MODEL
POOL_SIZES = (2, 4, 8, 16)
N_POOL_GROUPS = len(POOL_SIZES)
POOL_GROUP = POOL_WIDTH // N_POOL_GROUPS
ODD_IN = 2 * POOL_WIDTH
N_EVEN = (DEPTH_2 + 1) // 2
N_ODD = DEPTH_2 // 2


def _rmsnorm(x, g):
    xf = x.astype(jnp.float32)
    y = xf * lax.rsqrt(jnp.mean(xf * xf, axis=-1, keepdims=True) + EPS)
    return (y * g.astype(jnp.float32)).astype(x.dtype)

def _modulation(cvec, w, b):
    m = jax.nn.silu(cvec) @ w + b
    m = m[..., None, :]
    return m[..., :D_MODEL], m[..., D_MODEL:2 * D_MODEL], m[..., 2 * D_MODEL:]

def _axial_rope(rows):
    row = jnp.broadcast_to(jnp.arange(rows)[:, None], (rows, GRID_W)).reshape(-1).astype(jnp.float32)
    col = jnp.broadcast_to(jnp.arange(GRID_W)[None, :], (rows, GRID_W)).reshape(-1).astype(jnp.float32)
    inv = ROPE_THETA ** (-jnp.arange(AXIS_FREQS, dtype=jnp.float32) / AXIS_FREQS)
    ang = jnp.concatenate([row[:, None] * inv, col[:, None] * inv], axis=-1)
    return jnp.cos(ang), jnp.sin(ang)

def _rope(x, cos, sin):
    shape = (cos.shape[0],) + (1,) * (x.ndim - 3) + (cos.shape[1],)
    cos = cos.reshape(shape)
    sin = sin.reshape(shape)
    xf = x.astype(jnp.float32)
    x1, x2 = xf[..., :HALF_DIM], xf[..., HALF_DIM:]
    return jnp.concatenate([x1 * cos - x2 * sin, x2 * cos + x1 * sin], axis=-1).astype(x.dtype)

def _split_kv(kv):
    B, L = kv.shape[:2]
    kA = kv[..., :KV_A_W].reshape(B, L, N_KV_A, HEAD_DIM)
    vA = kv[..., KV_A_W:2 * KV_A_W].reshape(B, L, N_KV_A, HEAD_DIM)
    kB = kv[..., 2 * KV_A_W:2 * KV_A_W + KV_B_W].reshape(B, L, N_KV_B, HEAD_DIM)
    vB = kv[..., 2 * KV_A_W + KV_B_W:].reshape(B, L, N_KV_B, HEAD_DIM)
    return kA, vA, kB, vB

def _split_q(q):
    B, L = q.shape[:2]
    q = q.reshape(B, L, N_HEADS_A + N_HEADS_B, HEAD_DIM)
    qA = q[:, :, :N_HEADS_A].reshape(B, L, N_KV_A, G_A, HEAD_DIM)
    qB = q[:, :, N_HEADS_A:].reshape(B, L, N_KV_B, G_B, HEAD_DIM)
    return qA, qB

def _dense_attention(q, k, v):
    B, L = q.shape[:2]
    nb = L // Q_BLOCK

    def block(n):
        qb = lax.dynamic_slice_in_dim(q, n * Q_BLOCK, Q_BLOCK, axis=1)
        s = jnp.einsum('bqkgd,bskd->bkgqs', qb, k).astype(jnp.float32) * ATTN_SCALE
        p = jax.nn.softmax(s, axis=-1).astype(v.dtype)
        return jnp.einsum('bkgqs,bskd->bqkgd', p, v)

    o = lax.map(block, jnp.arange(nb))
    return jnp.moveaxis(o, 0, 1).reshape(B, L, -1)

def _window_attention(q, k, v, kc, vc, sink):
    B, L, KV, G, _ = q.shape
    C = kc.shape[1]
    nb = L // Q_BLOCK
    pad = ((0, 0), (WINDOW_2, WINDOW_2), (0, 0), (0, 0))
    kp = jnp.pad(k, pad)
    vp = jnp.pad(v, pad)
    sink_l = sink.astype(jnp.float32).reshape(1, KV, G, 1, 1)

    def block(n):
        start = n * Q_BLOCK
        qb = lax.dynamic_slice_in_dim(q, start, Q_BLOCK, axis=1)
        kb = lax.dynamic_slice_in_dim(kp, start, BAND, axis=1)
        vb = lax.dynamic_slice_in_dim(vp, start, BAND, axis=1)
        qpos = start + jnp.arange(Q_BLOCK)
        kpos = start - WINDOW_2 + jnp.arange(BAND)
        valid = (jnp.abs(kpos[None, :] - qpos[:, None]) <= WINDOW_2) & (kpos >= 0)[None, :] & (kpos < L)[None, :]
        s_band = jnp.einsum('bqkgd,bjkd->bkgqj', qb, kb).astype(jnp.float32) * ATTN_SCALE
        s_band = jnp.where(valid, s_band, NEG_INF)
        s_ctx = jnp.einsum('bqkgd,bckd->bkgqc', qb, kc).astype(jnp.float32) * ATTN_SCALE
        s_sink = jnp.broadcast_to(sink_l, s_ctx.shape[:-1] + (1,))
        p = jax.nn.softmax(jnp.concatenate([s_band, s_ctx, s_sink], axis=-1), axis=-1).astype(v.dtype)
        return (jnp.einsum('bkgqj,bjkd->bqkgd', p[..., :BAND], vb)
                + jnp.einsum('bkgqc,bckd->bqkgd', p[..., BAND:BAND + C], vc))

    o = lax.map(block, jnp.arange(nb))
    return jnp.moveaxis(o, 0, 1).reshape(B, L, -1)

def _ctx_attention(q, k, v, sink=None):
    B, C = q.shape[:2]
    s = jnp.einsum('bqkgd,bckd->bkgqc', q, k).astype(jnp.float32) * ATTN_SCALE
    if sink is not None:
        KV, G = q.shape[2], q.shape[3]
        s_sink = jnp.broadcast_to(sink.astype(jnp.float32).reshape(1, KV, G, 1, 1), s.shape[:-1] + (1,))
        p = jax.nn.softmax(jnp.concatenate([s, s_sink], axis=-1), axis=-1)[..., :C]
    else:
        p = jax.nn.softmax(s, axis=-1)
    return jnp.einsum('bkgqc,bckd->bqkgd', p.astype(v.dtype), v).reshape(B, C, -1)

def _attention_layer(x, ctx, cos, sin, c, c_ctx, mod_w, mod_b, pre_g, post_g, w_in, q_norm, k_norm, sink, w_out, need_ctx_out):
    shift, scale, gate = _modulation(c, mod_w, mod_b)
    shift_c, scale_c, gate_c = _modulation(c_ctx, mod_w, mod_b)
    h = _rmsnorm(x, pre_g) * (1 + scale) + shift
    hc = _rmsnorm(ctx, pre_g) * (1 + scale_c) + shift_c

    proj = h @ w_in
    qA, qB = _split_q(proj[..., :Q_W])
    kA, vA, kB, vB = _split_kv(proj[..., Q_W:Q_W + KV_W])
    z = proj[..., Q_W + KV_W:]

    kA_c, vA_c, kB_c, vB_c = _split_kv(hc @ w_in[:, Q_W:Q_W + KV_W])
    kA_c = _rmsnorm(kA_c, k_norm)

    qA = _rope(_rmsnorm(qA, q_norm), cos, sin)
    kA = _rope(_rmsnorm(kA, k_norm), cos, sin)
    outA = _dense_attention(qA, jnp.concatenate([kA, kA_c], axis=1), jnp.concatenate([vA, vA_c], axis=1))

    outB = _window_attention(_rope(qB, cos, sin), _rope(kB, cos, sin), vB, kB_c, vB_c, sink)

    y = jnp.concatenate([outA, outB], axis=-1) * jax.nn.silu(z)
    x = x + gate * _rmsnorm(y @ w_out, post_g)

    if need_ctx_out:
        qA_c, qB_c = _split_q(hc @ w_in[:, :Q_W])
        z_c = hc @ w_in[:, Q_W + KV_W:]
        oA_c = _ctx_attention(_rmsnorm(qA_c, q_norm), kA_c, vA_c)
        oB_c = _ctx_attention(qB_c, kB_c, vB_c, sink)
        yc = jnp.concatenate([oA_c, oB_c], axis=-1) * jax.nn.silu(z_c)
        ctx = ctx + gate_c * _rmsnorm(yc @ w_out, post_g)
    return x, ctx

def _multiscale_pool(u, pool_w, pool_scale):
    B, L, _ = u.shape
    uf = u.astype(jnp.float32)
    cs = jnp.concatenate([jnp.zeros_like(uf[:, :1]), lax.cumsum(uf, axis=1)], axis=1)
    t = jnp.arange(L)
    outs = []
    for g, w in enumerate(POOL_SIZES):
        lo = jnp.clip(t - w // 2, 0, L)
        hi = jnp.clip(t + w // 2, 0, L)
        csg = cs[..., g * POOL_GROUP:(g + 1) * POOL_GROUP]
        mean = (jnp.take(csg, hi, axis=1) - jnp.take(csg, lo, axis=1)) / (hi - lo).astype(jnp.float32)[:, None]
        outs.append(mean - uf[..., g * POOL_GROUP:(g + 1) * POOL_GROUP])
    pooled = jnp.stack(outs, axis=2).astype(u.dtype)
    mixed = jnp.einsum('blgc,gcd->blgd', pooled, pool_w).reshape(B, L, POOL_WIDTH)
    return mixed * pool_scale

def _pool_layer(x, ctx, c, c_ctx, mod_w, mod_b, pre_g, post_g, w_in, pool_w, pool_scale, w_out, need_ctx_out):
    shift, scale, gate = _modulation(c, mod_w, mod_b)
    h = _rmsnorm(x, pre_g) * (1 + scale) + shift
    proj = h @ w_in
    y = _multiscale_pool(proj[..., :POOL_WIDTH], pool_w, pool_scale) * jax.nn.silu(proj[..., POOL_WIDTH:])
    x = x + gate * _rmsnorm(y @ w_out, post_g)
    if need_ctx_out:
        shift_c, scale_c, gate_c = _modulation(c_ctx, mod_w, mod_b)
        hc = _rmsnorm(ctx, pre_g) * (1 + scale_c) + shift_c
        pc = hc @ w_in
        yc = _multiscale_pool(pc[..., :POOL_WIDTH], pool_w, pool_scale) * jax.nn.silu(pc[..., POOL_WIDTH:])
        ctx = ctx + gate_c * _rmsnorm(yc @ w_out, post_g)
    return x, ctx

def second_inputs(seed: int = 0) -> dict:
    key = jax.random.key(seed)
    ks = jax.random.split(key, 24)
    f32 = jnp.float32

    def nrm(k, shape, s):
        return jax.random.normal(k, shape, f32) * s

    return {
        'x': nrm(ks[0], (BATCH, SEQ, D_MODEL), 1.0),
        'c': nrm(ks[1], (BATCH, D_MODEL), 1.0),
        'ctx': nrm(ks[2], (BATCH, CTX_LEN, D_MODEL), 1.0),
        'c_ctx': nrm(ks[3], (D_MODEL,), 1.0),
        'ev_mod_w': nrm(ks[4], (N_EVEN, D_MODEL, 3 * D_MODEL), 0.5 * D_MODEL ** -0.5),
        'ev_mod_b': nrm(ks[5], (N_EVEN, 3 * D_MODEL), 0.02),
        'ev_pre_g': 1.0 + nrm(ks[6], (N_EVEN, D_MODEL), 0.05),
        'ev_post_g': 1.0 + nrm(ks[7], (N_EVEN, D_MODEL), 0.05),
        'ev_w_in': nrm(ks[8], (N_EVEN, D_MODEL, EVEN_IN), D_MODEL ** -0.5),
        'ev_q_norm': 1.0 + nrm(ks[9], (N_EVEN, HEAD_DIM), 0.05),
        'ev_k_norm': 1.0 + nrm(ks[10], (N_EVEN, HEAD_DIM), 0.05),
        'ev_sink': nrm(ks[11], (N_EVEN, N_HEADS_B), 0.5),
        'ev_w_out': nrm(ks[12], (N_EVEN, ATTN_WIDTH, D_MODEL), ATTN_WIDTH ** -0.5),
        'od_mod_w': nrm(ks[13], (N_ODD, D_MODEL, 3 * D_MODEL), 0.5 * D_MODEL ** -0.5),
        'od_mod_b': nrm(ks[14], (N_ODD, 3 * D_MODEL), 0.02),
        'od_pre_g': 1.0 + nrm(ks[15], (N_ODD, D_MODEL), 0.05),
        'od_post_g': 1.0 + nrm(ks[16], (N_ODD, D_MODEL), 0.05),
        'od_w_in': nrm(ks[17], (N_ODD, D_MODEL, ODD_IN), D_MODEL ** -0.5),
        'od_pool_w': nrm(ks[18], (N_ODD, N_POOL_GROUPS, POOL_GROUP, POOL_GROUP), POOL_GROUP ** -0.5),
        'od_pool_scale': 1.0 + nrm(ks[19], (N_ODD, POOL_WIDTH), 0.1),
        'od_w_out': nrm(ks[20], (N_ODD, POOL_WIDTH, D_MODEL), POOL_WIDTH ** -0.5),
    }

def second_block(x, c, ctx, c_ctx, ev_mod_w, ev_mod_b, ev_pre_g, ev_post_g, ev_w_in, ev_q_norm, ev_k_norm, ev_sink, ev_w_out,
              od_mod_w, od_mod_b, od_pre_g, od_post_g, od_w_in, od_pool_w, od_pool_scale, od_w_out):
    ROWS = x.shape[1] // GRID_W
    cos, sin = _axial_rope(ROWS)
    for i in range(DEPTH_2):
        need_ctx_out = any(j % 2 == 0 for j in range(i + 1, DEPTH_2))
        if i % 2 == 0:
            e = i // 2
            x, ctx = _attention_layer(x, ctx, cos, sin, c, c_ctx, ev_mod_w[e], ev_mod_b[e], ev_pre_g[e], ev_post_g[e],
                                      ev_w_in[e], ev_q_norm[e], ev_k_norm[e], ev_sink[e], ev_w_out[e], need_ctx_out)
        else:
            o = i // 2
            x, ctx = _pool_layer(x, ctx, c, c_ctx, od_mod_w[o], od_mod_b[o], od_pre_g[o], od_post_g[o],
                                 od_w_in[o], od_pool_w[o], od_pool_scale[o], od_w_out[o], need_ctx_out)
    return x


def setup_inputs(seed=0):
    out = dict(first_inputs(seed))
    for name, value in second_inputs(seed + 1).items():
        if name != "x":
            out[name + "_2"] = value
    return out


def reference(
    x, attn_norm_g, w_in, gla_conv_w, gla_gate_w2, gla_gate_b, gla_norm_g, nsa_q_norm_g,
    nsa_kc_norm_g, nsa_ks_norm_g, nsa_kw_norm_g, cmp_k_pos, cmp_k_w1, cmp_k_w2, cmp_v_pos,
    cmp_v_w1, cmp_v_w2, w_out, ffn_norm_g, w_gate, w_up, w_down, c_2, ctx_2, c_ctx_2,
    ev_mod_w_2, ev_mod_b_2, ev_pre_g_2, ev_post_g_2, ev_w_in_2, ev_q_norm_2, ev_k_norm_2,
    ev_sink_2, ev_w_out_2, od_mod_w_2, od_mod_b_2, od_pre_g_2, od_post_g_2, od_w_in_2,
    od_pool_w_2, od_pool_scale_2, od_w_out_2,
):
    x = first_block(
        x, attn_norm_g, w_in, gla_conv_w, gla_gate_w2, gla_gate_b, gla_norm_g, nsa_q_norm_g,
        nsa_kc_norm_g, nsa_ks_norm_g, nsa_kw_norm_g, cmp_k_pos, cmp_k_w1, cmp_k_w2, cmp_v_pos,
        cmp_v_w1, cmp_v_w2, w_out, ffn_norm_g, w_gate, w_up, w_down,
    )
    return second_block(
        x, c_2, ctx_2, c_ctx_2, ev_mod_w_2, ev_mod_b_2, ev_pre_g_2, ev_post_g_2, ev_w_in_2,
        ev_q_norm_2, ev_k_norm_2, ev_sink_2, ev_w_out_2, od_mod_w_2, od_mod_b_2, od_pre_g_2,
        od_post_g_2, od_w_in_2, od_pool_w_2, od_pool_scale_2, od_w_out_2,
    )


_drawn_inputs = setup_inputs


def setup_inputs(seed=0):
    import zlib

    import numpy as np

    out = dict(_drawn_inputs(seed))
    spreads = {}
    factors = {'attn_norm_g': 4.352,
     'gla_gate_w2': 3.897,
     'gla_gate_b': 64.0,
     'gla_norm_g': 6.178,
     'nsa_q_norm_g': 8.0,
     'nsa_kc_norm_g': 46.251,
     'nsa_ks_norm_g': 8.0,
     'nsa_kw_norm_g': 8.0,
     'cmp_k_pos': 8.0,
     'ffn_norm_g': 10.877,
     'ev_pre_g_2': 3.793,
     'ev_post_g_2': 200.0,
     'ev_q_norm_2': 28.233,
     'ev_k_norm_2': 25.368,
     'ev_sink_2': 8.0,
     'od_mod_b_2': 9.674,
     'od_pre_g_2': 142.291,
     'od_post_g_2': 200.0,
     'cmp_v_pos': 8.0,
     'ev_mod_b_2': 4.012,
     'od_pool_scale_2': 22.47}
    for name, (base, spread) in spreads.items():
        noise = np.random.default_rng([zlib.crc32(name.encode()), seed]).standard_normal(out[name].shape)
        drawn = base * np.exp(spread * noise) if base else spread * noise
        out[name] = __import__('jax').numpy.asarray(drawn.astype(out[name].dtype))
    for name, factor in factors.items():
        out[name] = (out[name] * factor).astype(out[name].dtype)
    return out
```

```python
from contextlib import ExitStack

import numpy as np
import concourse.bass as bass
from concourse import mybir

F32 = mybir.dt.float32
F32R = mybir.dt.float32r
ACT = mybir.ActivationFunctionType
ALU = mybir.AluOpType
AX = mybir.AxisListType

P = 128
T = 256
TT = T // P
D = 2048
DT = D // P
EPS = 1e-6
NEG = -1e30
HALF = 8 * P
DH = 128
GLA_H, GLA_DV = 4, 256
CHUNK, TAU = 64, 16.0
NSA_H, CMP_W, CMP_STRIDE = 8, 32, 16
N_CMP = (T - CMP_W) // CMP_STRIDE + 1
FFN_TILES = 5632 // P
CHUNKS = (16, 16, 12)
assert sum(CHUNKS) == FFN_TILES
SCALE = DH ** -0.5

QT, KT, VT, GOUT = 0, 4, 8, 16
NQ, NKS, NKW, NKC, NVC, NVS, NVW, LAST = 24, 32, 34, 36, 38, 40, 42, 44
GATE_ROW = 32

STAGES = [("conv", 16), ("rest", 29), ("out", 16),
          ("up0", 32), ("down0", 16), ("up1", 32), ("down1", 16), ("up2", 24), ("down2", 16),
          ("ev_kv", 8), ("ev_q", 16), ("ev_z", 16), ("ev_out", 16),
          ("od_u", 16), ("pool", 4), ("od_z", 16), ("od_out", 16)]
FIRST, COUNT = {}, {}
_s = 0
for _n, _c in STAGES:
    FIRST[_n], COUNT[_n] = _s, _c
    _s += _c
STEPS = _s
HALVES = 2 * STEPS
CMP_HALVES = 4
MOD_TILES = 96
SIDE_HALVES = 2 * CMP_HALVES + 2 * MOD_TILES
MODS_FIRST = 8

COLS = {}
_o = 0
for _n, _w in [("attn_g", 16), ("conv", 64), ("gate_b", 4), ("gla_g", 2), ("q_g", 1), ("kc_g", 1),
               ("ks_g", 1), ("kw_g", 1), ("k_pos", 32), ("v_pos", 32), ("ffn_g", 16), ("ev_pre", 16),
               ("ev_post", 16), ("od_pre", 16), ("od_post", 16), ("pool_s", 16), ("mod_b", 96),
               ("cvec", 32), ("ev_qn", 1), ("ev_kn", 1), ("sink", 8)]:
    COLS[_n] = (_o, _w)
    _o += _w
NCOLS = _o

CONS = {}
_o = 0
for _n, _w in [("ident", P), ("ones", P), ("above", P), ("below", P), ("rot", P), ("cos", T), ("sin", T),
               ("cmp_add", TT * N_CMP), ("cmp_ok", TT * N_CMP)]:
    CONS[_n] = (_o, _w)
    _o += _w
NCONS = _o
LEVELS = 6
TABLE = 4 * T


def steps(eng, stage, body, first=0, last=0):
    n = COUNT[stage]
    for k in range(first):
        body(0, k)
    pairs = (n - first - last) // 2
    with eng.Fori(0, pairs) as i:
        body(i, first)
        body(i, first + 1)
    for k in range(first + 2 * pairs, n):
        body(0, k)


def dve_reads(stage):
    n = 0
    for name, count in STAGES:
        if name == stage:
            return n
        n += 0 if name[:2] == "up" or name[-2:] == "_z" else count


ROPE_PAIRS = [0, 4] + list(range(16, 32, 2))


def build(nc, x, ctx_in, w_main, w_side, cols_in, cons_in, gla_masks_in, counts_in, gate_w2_in, cmp_w2_in, out):
    stack = ExitStack()
    with stack:
        K = 1024
        sems = {}

        def S(name):
            if name not in sems:
                sems[name] = stack.enter_context(nc.semaphore(name))
            return sems[name]

        start = -(-nc.sbuf_base // 64) * 64

        def at(name, offset, shape, dtype=F32):
            return nc.alloc_sbuf_tensor_at(name, shape, dtype, offset=start + offset)

        RAW, HI, LO, SIDE, RES, A, B, PR, CO = (0, 16 * K, 32 * K, 48 * K, 64 * K, 80 * K, 112 * K, 144 * K, 189 * K)
        raw = at("raw", RAW, [P, 4, HALF])
        w_hi = at("w_hi", HI, [P, 4, HALF], F32R)
        w_lo = at("w_lo", LO, [P, 4, HALF], F32R)
        side = at("side", SIDE, [P, 4, HALF])
        res = at("res", RES, [P, DT, T])
        a_hi = at("a_hi", A, [P, 16, T], F32R)
        a_lo = at("a_lo", A + 16 * K, [P, 16, T], F32R)
        b_hi = at("b_hi", B, [P, 16, T], F32R)
        b_lo = at("b_lo", B + 16 * K, [P, 16, T], F32R)
        pr = at("pr", PR, [P, 45, T])
        place = [CO]

        def small(name, shape):
            n = 4
            for d in shape[1:]:
                n *= d
            place[0] += -(-n // 32) * 32
            return at(name, place[0] - -(-n // 32) * 32, shape)

        cons = small("cons", [P, NCONS])
        cols = small("cols", [P, NCOLS])
        table = small("table", [P, TABLE])
        gate_w2 = small("gate_w2", [P, 512])
        cmp_w2 = small("cmp_w2", [P, 2, P])
        rstd = small("rstd", [P, T])
        csil = small("csil", [P, 16, 2])
        mods = small("mods", [P, MOD_TILES, 2])
        ev_gain = small("ev_gain", [P, 16, 2])
        od_gain = small("od_gain", [P, 16])
        ev_gate = small("ev_gate", [P, 16])
        od_gate = small("od_gate", [P, 16])
        neg_sink = small("neg_sink", [P, 8])
        at_max = small("at_max", [P, 16])
        at_nb = small("at_nb", [P, 16])
        at_den = small("at_den", [P, 16])
        at_coef = small("at_coef", [P, 16])
        at_sink = small("at_sink", [P, 8])
        x_tok = at("x_tok", B, [P, TT, D])
        sq = at("sq", PR, [P, 16, T])
        sq2 = at("sq2", PR + 16 * K, [P, 16, T])
        ctx_f = at("ctx_f", PR, [P, DT, T])
        g_b = at("g_b", A, [P, 4, T])
        g_d = at("g_d", A + 4 * K, [P, 4, T])
        g_q = at("g_q", A + 8 * K, [P, 4, T])
        g_k = at("g_k", A + 12 * K, [P, 4, T])
        g_qe = at("g_qe", A + 16 * K, [P, 4, T])
        g_kd = at("g_kd", A + 20 * K, [P, 4, T])
        g_keep = at("g_keep", A + 24 * K, [P, 4, T])
        g_sc = at("g_sc", A + 28 * K, [P, TT, 4, P])
        v_tok = at("v_tok", B, [P, TT, 1024])
        k_tok = at("k_tok", B + 8 * K, [P, TT, 512])
        state = at("state", B + 12 * K, [P, 3, 1024])
        g_tmp = at("g_tmp", B + 24 * K, [P, TT, 4, P])
        g_el = at("g_el", B + 28 * K, [P, 4, 4])
        g_sq = at("g_sq", A, [P, 4, 2, T])
        g_rs = at("g_rs", A + 8 * K, [P, 4, T])
        g_y = at("g_y", A + 12 * K, [P, 8, T])
        n_sq = at("n_sq", A, [P, 12, T])
        n_rs = at("n_rs", A + 12 * K, [P, 12, T])
        n_x = at("n_x", A + 24 * K, [P, 2, CMP_W, 2 * N_CMP])
        prob = at("prob", A, [P, 8, 2, T])
        prob_t = at("prob_t", A + 16 * K, [P, 2, 5, P])
        v_nsa = at("v_nsa", B + 24 * K, [P, TT, 4, P])
        n_small = B + 8 * K
        hid = at("hid", n_small, [P, 2 * 2 * N_CMP])
        c_sq = at("c_sq", n_small + 256, [P, 2 * N_CMP])
        c_rs = at("c_rs", n_small + 384, [P, 2 * N_CMP])
        k_cmp = at("k_cmp", n_small + 512, [P, 2 * N_CMP])
        v_cmp = at("v_cmp", n_small + 640, [N_CMP, 2, P])
        gates = at("gates", n_small + 1664, [P, TT, 24])
        c_s = at("c_s", n_small + 1856, [P, TT, 8, N_CMP])
        c_mx = at("c_mx", n_small + 2816, [P, TT, 8])
        c_den = at("c_den", n_small + 2880, [P, TT, 8])
        c_p = at("c_p", n_small + 2944, [P, TT, 8, N_CMP])
        sg = at("sg", PR + 40 * K, [P, 2, T])
        gated = at("gated", PR + 42 * K, [P, 2, T])
        e_sq = at("e_sq", B, [P, 12, T])
        e_rs = at("e_rs", B + 12 * K, [P, 12, T])
        e_rot = at("e_rot", B + 24 * K, [P, 2, 2, T])
        prob2 = at("prob2", B, [P, 8, 2, T])
        prob2_t = at("prob2_t", B + 16 * K, [P, 2, 5, P])
        v_ev = at("v_ev", B + 22 * K, [P, 2, TT, 4, P])
        f_a = at("f_a", PR + 16 * K, [P, 4, T + 8])
        f_b = at("f_b", PR + 21 * K, [P, 4, T + 8])
        pooled = at("pooled", PR + 26 * K, [P, 16, T])
        o_tok = at("o_tok", B, [P, TT, D])

        ps = stack.enter_context(nc.psum_tensor("ps", [P, 8, 512], F32))

        def con(name):
            a, w = CONS[name]
            return cons[:, a:a + w]

        def col(name, j=0, n=1):
            a, _ = COLS[name]
            return cols[:, a + j:a + j + n]

        def cbc(ap, n):
            return ap.rearrange("p (a w) -> p a w", a=1).to_broadcast([ap.shape[0], n, ap.shape[1]])

        def vbc(ap, n):
            return ap.rearrange("p (w a) -> p w a", a=1).to_broadcast([ap.shape[0], ap.shape[1], n])

        ident, ones = con("ident"), con("ones")

        raw_full = [S(f"raw_full{j}") for j in range(4)]
        side_full = [S(f"side_full{j}") for j in range(4)]
        hi_ready = S("hi_ready")
        lo_ready = S("lo_ready")
        halves_used = S("halves_used")
        side_used = S("side_used")
        dve_read = S("dve_read")
        silu_ready = S("silu_ready")

        ATT = {"n0": 0, "n1": 1, "a0": 2, "a1": 3, "b0": 4, "b1": 5}

        def att(name):
            kind, tt = name[0], int(name[1])
            a = {"kind": kind, "tt": tt, "base": 8 * ATT[name], "cols": slice(tt * P, tt * P + P)}
            if kind == "n":
                a["q"] = lambda h: NQ + h
                a["k"] = lambda h, part: (NKS, NKW)[part] + h // 4
                a["keys"] = (tt + 1) * P
                a["mask"] = [(part, tt, "above") for part in range(2)]
                a["v"] = lambda h, part, b: v_nsa[:, b, 2 * part + h // 4, :]
                a["prob"], a["prob_t"] = prob, prob_t
            else:
                off = 0 if kind == "a" else 4
                a["q"] = lambda h: 16 + 2 * off + h
                a["k"] = lambda h, part: 8 * part + off + h // 4
                a["keys"] = T
                a["mask"] = [] if kind == "a" else [(0, 1 - tt, "above" if tt == 0 else "below")]
                a["v"] = lambda h, part, b: v_ev[:, part, b, off // 2 + h // 4, :]
                a["prob"], a["prob_t"] = prob2, prob2_t
            a["blocks"] = [(part, b) for part in range(2) for b in range(a["keys"] // P)]
            return a

        block = stack.enter_context(nc.Block())

        @block.sync
        def _(sp):
            sp.dma_start(cons[:, :], cons_in).then_inc(S("const_in"), 16)
            sp.dma_start(cols[:, :], cols_in).then_inc(S("const_in"), 16)
            sp.dma_start(x_tok[:, :, :], x.rearrange("(a p) d -> p a d", p=P)).then_inc(S("x_in"), 16)
            for h in range(4):
                sp.dma_start(raw[:, h, :], w_main[h]).then_inc(raw_full[h], 16)
            sp.dma_start(table[:, 0:7 * P], gla_masks_in).then_inc(S("small_in"), 16)
            sp.dma_start(gate_w2[0:16, :], gate_w2_in).then_inc(S("small_in"), 16)
            sp.dma_start(cmp_w2[:, :, :], cmp_w2_in).then_inc(S("small_in"), 16)

            def load(i, h):
                sp.wait_ge(lo_ready, i * 4 + (h - 3))
                sp.dma_start(raw[:, h % 4, :], w_main[bass.ds(i * 4 + h, 1)].rearrange("a p n -> (a p) n"))\
                  .then_inc(raw_full[h % 4], 16)

            def loads(h0, h1):
                whole = (h1 - h0) // 4
                with sp.Fori(0, whole) as i:
                    for c in range(4):
                        load(i, h0 + c)
                for h in range(h0 + 4 * whole, h1):
                    sp.wait_ge(lo_ready, h - 3)
                    sp.dma_start(raw[:, h % 4, :], w_main[h]).then_inc(raw_full[h % 4], 16)

            h_ctx = 2 * FIRST["ev_kv"] + 2
            loads(4, h_ctx)
            sp.wait_ge(dve_read, dve_reads("ev_kv"))
            sp.dma_start(x_tok[:, :, :], ctx_in.rearrange("(a p) d -> p a d", p=P)).then_inc(S("ctx_in"), 16)
            sp.dma_start(table[:, :], counts_in).then_inc(S("counts_in"), 16)
            loads(h_ctx, HALVES)
            for tt in range(TT):
                sp.wait_ge(S(f"o_tok{tt}_a"), 2)
                sp.wait_ge(S(f"o_tok{tt}_d"), 2)
                sp.dma_start(out[tt * P:(tt + 1) * P, :], o_tok[:, tt, :]).then_inc(S("stored"), 16)
            sp.wait_ge(S("stored"), 16 * TT)

        @block.gpsimd
        def _(pool):
            for h in range(4):
                pool.dma_start(side[:, h, :], w_side[h]).then_inc(side_full[h], 16)
            with pool.Fori(0, SIDE_HALVES // 4 - 1) as i:
                for c in range(4):
                    pool.wait_ge(side_used, i * 4 + (c + 1))
                    pool.dma_start(side[:, c, :], w_side[bass.ds(i * 4 + (4 + c), 1)].rearrange("a p n -> (a p) n"))\
                        .then_inc(side_full[c], 16)

        @block.tensor
        def _(pe):
            def half_products(out_ap, c, par, blocks, act_hi, act_lo, tile0, first, last):
                slot = 2 * par + c
                for n, b in enumerate(blocks):
                    wh, wl = w_hi[:, slot, b * P:(b + 1) * P], w_lo[:, slot, b * P:(b + 1) * P]
                    kt = tile0 + n
                    pe.matmul(out_ap, wh, act_hi[:, kt, :], start=first and n == 0, stop=False)
                    pe.matmul(out_ap, wh, act_lo[:, kt, :], start=False, stop=False)
                    mm = pe.matmul(out_ap, wl, act_hi[:, kt, :], start=False, stop=last and n == len(blocks) - 1)
                return mm

            def step(stage, i, k, act, kt=16, free=None, second=None):
                s = FIRST[stage] + k
                par = s % 2
                if free is not None:
                    pe.wait_ge(*free)
                for c in range(2):
                    pe.wait_ge(lo_ready, i * 4 + (2 * s + c + 1))
                    nb = min(8, kt - 8 * c)
                    mm = half_products(ps[:, par, 0:T], c, par, range(nb), *act, 8 * c, c == 0, c == 1)
                    if second is not None:
                        mm = half_products(ps[:, 2 + par, 0:T], c, par, range(nb), *second, 8 * c, c == 0, c == 1)
                    mm.then_inc(halves_used, 1)

            def run(stage, act, kt=16, second=None, first=0):
                base = dve_reads(stage)

                def body(i, k):
                    step(stage, i, k, act, kt, None if base + k < 2 else (dve_read, i * 2 + (base + k - 1)), second)
                steps(pe, stage, body, first=first)

            def run_z(stage, done):
                def body(i, k):
                    step(stage, i, k, (a_hi, a_lo), free=(silu_ready, i * 2 + (FFN_TILES + done + k)))
                steps(pe, stage, body)

            def mod(i, m):
                dst = ps[:, 7, 2 * m:2 * m + 2] if isinstance(i, int) else ps[:, 7, bass.ds(i * 4 + 2 * m, 2)]
                for c in range(2):
                    h = 2 * CMP_HALVES + 2 * m + c
                    pe.wait_ge(side_full[h % 4], i * 16 + 16 * (h // 4 + 1))
                    for b in range(8):
                        kt = 8 * c + b
                        mm = pe.matmul(dst, side[:, h % 4, b * P:(b + 1) * P], csil[:, kt, :],
                                       start=kt == 0, stop=kt == 15)
                    mm.then_inc(side_used, 1)

            def turn(src_ap, bank, at_col, rows=P, ncols=P, base=0):
                return pe.transpose(ps[0:ncols, bank, at_col:at_col + rows], src_ap, ident[base:base + rows, base:base + rows])

            def norm(name, bank=2):
                for q in range(4):
                    pe.wait_ge(S(f"{name}_sq"), q + 1)
                    for f in range(4 * q, 4 * q + 4):
                        src = sq2 if name in ("ctx", "ev_post", "od_post") else sq
                        mm = pe.matmul(ps[:, bank, 0:T], ones, src[:, f, :], start=f == 0, stop=f == 15)
                mm.then_inc(S(f"{name}_ms"), 1)

            def token_to_feature(name):
                for g in range(8):
                    for f in range(2 * g, 2 * g + 2):
                        for tt in range(TT):
                            mm = turn(x_tok[:, tt, f * P:(f + 1) * P], g, (f % 2) * T + tt * P)
                    mm.then_inc(S(f"{name}_t"), 1)

            pe.wait_ge(S("const_in"), 32)
            pe.wait_ge(S("x_in"), 16)
            token_to_feature("x")
            norm("attn")
            pe.wait_ge(S("attn_lo"), 16)
            run("conv", (a_hi, a_lo), first=2)
            run("rest", (a_hi, a_lo))

            pe.wait_ge(S("small_in"), 48)
            pe.wait_ge(dve_read, dve_reads("out"))
            for h in range(4):
                mm = pe.matmul(ps[:, 2 + h // 2, (h % 2) * T:(h % 2 + 1) * T], gate_w2[0:16, h * P:(h + 1) * P],
                               pr[0:16, LAST, :], start=True, stop=True)
            mm.then_inc(S("g_z"), 1)

            def gla_scores(q, k):
                for tt in range(TT):
                    for h in range(4):
                        mm = pe.matmul(ps[:, 4 + tt, h * P:(h + 1) * P], k(h)[:, tt * P:(tt + 1) * P],
                                       q(h)[:, tt * P:(tt + 1) * P], start=True, stop=True)
                return mm

            pe.wait_ge(S("g_silu"), 2)
            gla_scores(lambda h: pr[:, QT + h, :], lambda h: pr[:, KT + h, :]).then_inc(S("g_s"), 1)
            for tt in range(TT):
                for f in range(8):
                    mm = turn(pr[:, VT + f, tt * P:(tt + 1) * P], (0, 6)[tt] + f // 4, (f % 4) * P)
            mm.then_inc(S("g_vt"), 1)
            for lv in range(LEVELS):
                pe.wait_ge(S("g_mul"), 2 * (lv + 1))
                pe.wait_ge(S("g_msk"), 2 * (lv + 1))
                gla_scores(lambda h: g_q[:, h, :], lambda h: g_k[:, h, :]).then_inc(S("g_s"), 1)
            pe.wait_ge(S("g_kdr"), 1)
            for tt in range(TT):
                for h in range(4):
                    mm = turn(g_kd[:, h, tt * P:(tt + 1) * P], 2 + tt, h * P)
            mm.then_inc(S("g_kt"), 1)
            pe.wait_ge(S("g_ktok"), 1)
            pe.wait_ge(S("g_vtok"), 2)
            for c in range(3):
                tt, r0 = c // 2, (c % 2) * CHUNK
                for h in range(4):
                    mm = pe.matmul(ps[:, 2 * (c % 2) + h // 2, (h % 2) * 256:(h % 2 + 1) * 256],
                                   k_tok[r0:r0 + CHUNK, tt, h * P:(h + 1) * P],
                                   v_tok[r0:r0 + CHUNK, tt, h * 256:(h + 1) * 256], start=True, stop=True)
                mm.then_inc(S("g_kv"), 1)
                if c == 1:
                    pe.wait_ge(S("g_state"), 1)
            pe.wait_ge(S("g_state"), 3)
            pe.wait_ge(S("g_add"), 2 * LEVELS)
            for h in range(4):
                bank, started = (2, 3, 6, 7)[h], False
                for e in range(2):
                    rows = slice(h * 256 + e * P, h * 256 + (e + 1) * P)
                    for tt in range(TT):
                        o_ap = ps[:, bank, e * T + tt * P:e * T + (tt + 1) * P]
                        pe.matmul(o_ap, v_tok[:, tt, rows], g_sc[:, tt, h, :], start=not started, stop=False,
                                  skip_group_check=True)
                        started = True
                        for c in (2 * tt, 2 * tt + 1):
                            if c == 0:
                                continue
                            mm = pe.matmul(ps[:, bank, e * T + c * CHUNK:e * T + (c + 1) * CHUNK],
                                           state[:, c - 1, rows], g_qe[:, h, c * CHUNK:(c + 1) * CHUNK],
                                           start=False, stop=e == 1 and c == 3, skip_group_check=True)
                mm.then_inc(S("g_o"), 1)
            pe.wait_ge(S("g_sqr"), 4)
            for p2 in range(2):
                for e in range(2):
                    mm = pe.matmul(ps[:, 4 + p2, 0:2 * T], ones, g_sq[:, 2 * p2:2 * p2 + 2, e, :],
                                   start=e == 0, stop=e == 1)
            mm.then_inc(S("g_ms"), 1)

            pe.wait_ge(S("g_out"), 1)
            pe.wait_ge(S("n_sqr"), 1)
            for p2 in range(6):
                mm = pe.matmul(ps[:, p2, :], ones, n_sq[:, 2 * p2:2 * p2 + 2, :], start=True, stop=True)
            mm.then_inc(S("n_ms"), 1)
            for tt in range(TT):
                mm = turn(pr[GATE_ROW:GATE_ROW + 24, LAST, tt * P:(tt + 1) * P], 6, 32 * tt, rows=24, base=GATE_ROW)
            mm.then_inc(S("n_gt"), 1)
            pe.wait_ge(S("n_xr"), 2)
            for kv in range(2):
                for j in range(CMP_W):
                    idx = CMP_HALVES * kv + j // 8
                    if j % 8 == 0:
                        pe.wait_ge(side_full[idx % 4], 16 * (idx // 4 + 1))
                    mm = pe.matmul(ps[:, 7, 32 * kv:32 * kv + 2 * N_CMP],
                                   side[:, idx % 4, (j % 8) * P:(j % 8 + 1) * P], n_x[:, kv, j, :],
                                   start=j == 0, stop=j == CMP_W - 1)
                    if j % 8 == 7:
                        mm.then_inc(side_used, 1)
            pe.wait_ge(S("n_hs"), 1)
            pe.wait_ge(S("n_gs"), 1)
            mm = pe.matmul(ps[:, 6, 0:2 * N_CMP], cmp_w2[:, 0, :], hid[:, 0:2 * N_CMP], start=True, stop=True)
            mm.then_inc(S("n_kc"), 1)
            for kv in range(2):
                mm = pe.matmul(ps[0:N_CMP, 7, kv * P:(kv + 1) * P],
                               hid[:, (2 + kv) * N_CMP:(3 + kv) * N_CMP], cmp_w2[:, 1, :], start=True, stop=True)
            mm.then_inc(S("n_vc"), 1)
            pe.wait_ge(S("n_csq"), 1)
            pe.wait_ge(S("n_msr"), 1)
            mm = pe.matmul(ps[:, 2, 0:2 * N_CMP], ones, c_sq[:, :], start=True, stop=True)
            mm.then_inc(S("n_cms"), 1)
            for tt in range(TT):
                for f in range(4):
                    mm = turn(pr[:, NVS + f, tt * P:(tt + 1) * P], tt, f * P)
            mm.then_inc(S("n_vt"), 1)
            pe.wait_ge(S("n_qk"), 3)
            pe.wait_ge(S("n_kcn"), 1)
            for tt in range(TT):
                for h in range(8):
                    mm = pe.matmul(ps[:, 2 + tt, 16 * h:16 * h + N_CMP], pr[:, NQ + h, tt * P:(tt + 1) * P],
                                   k_cmp[:, (h // 4) * N_CMP:(h // 4 + 1) * N_CMP], start=True, stop=True)
            mm.then_inc(S("n_cs"), 1)

            def attend(name):
                a = att(name)
                base = a["base"]
                if base:
                    pe.wait_ge(S("at_out"), base)
                for h in range(8):
                    if h >= 4:
                        pe.wait_ge(S("at_exp"), base + h - 3)
                    for part in range(2):
                        mm = pe.matmul(ps[:, 2 + h % 4, part * T:part * T + a["keys"]],
                                       pr[:, a["q"](h), a["cols"]], pr[:, a["k"](h, part), 0:a["keys"]],
                                       start=True, stop=True)
                    mm.then_inc(S("at_sc"), 1)

                def values(h):
                    pe.wait_ge(S("at_pt"), base + h + 1)
                    if h >= 2:
                        pe.wait_ge(S("at_out"), base + h - 1)
                    blocks = a["blocks"]
                    for n, (part, b) in enumerate(blocks):
                        mm = pe.matmul(ps[:, 6 + h % 2, 0:P], a["v"](h, part, b), a["prob_t"][:, h % 2, n, :],
                                       start=n == 0, stop=a["kind"] != "n" and n == len(blocks) - 1)
                    if a["kind"] == "n":
                        mm = pe.matmul(ps[:, 6 + h % 2, 0:P], v_cmp[:, h // 4, :], a["prob_t"][0:N_CMP, h % 2, 4, :],
                                       start=False, stop=True)
                    mm.then_inc(S("at_pv"), 1)

                pe.wait_ge(S("at_exp"), base + 8)
                for h in range(8):
                    pe.wait_ge(S("at_scl"), base + h + 1)
                    if h >= 2:
                        pe.wait_ge(S("at_pt"), base + h - 1)
                    for n, (part, b) in enumerate(a["blocks"]):
                        mm = turn(a["prob"][:, h, part, b * P:(b + 1) * P], h % 2, n * P)
                    if a["kind"] == "n":
                        mm = turn(c_p[:, a["tt"], h, :], 2 + h % 2, 0, ncols=N_CMP)
                    mm.then_inc(S("at_t"), 1)
                    if h:
                        values(h - 1)
                values(7)

            pe.wait_ge(S("n_vtok"), 1)
            pe.wait_ge(S("c_ready"), 2)
            attend("n0")
            attend("n1")

            pe.wait_ge(S("mix_lo"), 1)
            run("out", (b_hi, b_lo))

            pe.wait_ge(S("csil"), 1)
            for m in range(MODS_FIRST):
                mod(0, m)
            norm("ffn")
            pe.wait_ge(S("ffn_lo"), 16)
            mod_at = MODS_FIRST
            for c, n in enumerate(CHUNKS):
                silus = sum(CHUNKS[:c])
                pe.wait_ge(dve_read, dve_reads(f"up{c}"))

                def body(i, k, c=c, silus=silus, m0=mod_at):
                    if k % 2 == 0:
                        step(f"up{c}", i, k, (a_hi, a_lo), free=(silu_ready, i + (silus + 1)))
                        mod(i, m0)
                    else:
                        step(f"up{c}", i, k, (a_hi, a_lo), free=(S("gate_y"), i + (silus + 1)))
                        mod(i, m0 + 1)
                steps(pe, f"up{c}", body)
                mod_at += n * 2
                pe.wait_ge(S("gate_lo"), silus + n)
                run(f"down{c}", (b_hi, b_lo), kt=n)
            assert mod_at == MOD_TILES

            pe.wait_ge(S("mods_read"), 1)
            norm("ev")
            pe.wait_ge(S("ctx_in"), 16)
            pe.wait_ge(S("ev_rs"), 3)
            token_to_feature("ctx")
            norm("ctx")
            pe.wait_ge(S("ev_lo"), 16)
            pe.wait_ge(S("ctx_lo"), 16)
            run("ev_kv", (a_hi, a_lo), second=(b_hi, b_lo))
            run("ev_q", (a_hi, a_lo))
            pe.wait_ge(S("e_sqr"), 3)
            for p2 in range(6):
                mm = pe.matmul(ps[:, 2 + p2, :], ones, e_sq[:, 2 * p2:2 * p2 + 2, :], start=True, stop=True)
            mm.then_inc(S("e_ms"), 1)
            pe.wait_ge(S("e_msr"), 1)
            for src in range(2):
                for tt in range(TT):
                    for f in range(4):
                        tile = 8 * src + (2, 3, 6, 7)[f]
                        mm = turn(pr[:, tile, tt * P:(tt + 1) * P], 4 + 2 * src + tt, f * P)
            mm.then_inc(S("e_vt"), 1)
            pe.wait_ge(S("e_nrm"), 3)
            for n, t0 in enumerate(ROPE_PAIRS):
                if n >= 4:
                    pe.wait_ge(S("e_rot"), n - 3)
                pe.matmul(ps[:, n % 4, :], con("rot"), pr[:, t0:t0 + 2, :], start=True, stop=True)\
                  .then_inc(S("e_rp"), 1)
            pe.wait_ge(S("e_rope"), len(ROPE_PAIRS))
            pe.wait_ge(S("e_vtok"), 4)
            for name in ("a0", "a1", "b0", "b1"):
                attend(name)
            pe.wait_ge(S("at_out"), 48)
            run_z("ev_z", 0)
            pe.wait_ge(S("gate_lo"), FFN_TILES + 16)
            run("ev_out", (b_hi, b_lo))
            norm("ev_post")

            norm("od")
            pe.wait_ge(S("od_lo"), 16)
            run("od_u", (a_hi, a_lo))
            pe.wait_ge(S("pool_lo"), 4)
            base = dve_reads("pool")
            for g in range(4):
                s = FIRST["pool"] + g
                par = s % 2
                if g >= 2:
                    pe.wait_ge(dve_read, base + g - 1)
                for c in range(2):
                    pe.wait_ge(lo_ready, 2 * s + c + 1)
                    for n in range(2):
                        mm = half_products(ps[:, 2 * par + c, n * T:(n + 1) * T], c, par, range(4 * n, 4 * n + 4),
                                           b_hi, b_lo, 4 * g, True, True)
                    mm.then_inc(halves_used, 1)
            pe.wait_ge(dve_read, base + 4)
            run_z("od_z", 16)
            pe.wait_ge(S("gate_lo"), FFN_TILES + 32)
            run("od_out", (b_hi, b_lo))
            norm("od_post")
            pe.wait_ge(S("final"), 1)
            for tt in range(TT):
                for g in range(4):
                    for f in range(4 * g, 4 * g + 4):
                        mm = turn(res[:, f, tt * P:(tt + 1) * P], 4 * tt + g, (f % 4) * P)
                    mm.then_inc(S("o_t"), 1)

        def gate_silu_steps(act, stage, silus):
            def extra(i, k):
                if k % 2:
                    return
                s = FIRST[stage] + k
                act.wait_ge(halves_used, i * 4 + (2 * s + 2))
                act.wait_ge(S("gate_y"), i + (silus + 1))
                act.activation(sg[:, 0, :], ps[:, s % 2, 0:T], ACT.Silu).then_inc(silu_ready, 1)
            return extra

        def z_silu_steps(act, stage, done):
            def extra(i, k):
                s = FIRST[stage] + k
                act.wait_ge(halves_used, i * 4 + (2 * s + 2))
                act.wait_ge(S("gate_y"), i * 2 + (FFN_TILES + done + k + 1))
                act.activation(sg[:, 0, :], ps[:, s % 2, 0:T], ACT.Silu).then_inc(silu_ready, 1)
            return extra

        @block.scalar
        def _(act):
            def hi(i, s):
                for c in range(2):
                    slot = 2 * (s % 2) + c
                    act.wait_ge(raw_full[slot], i * 16 + 16 * (s // 2 + 1))
                    if s >= 2:
                        act.wait_ge(halves_used, i * 4 + (2 * s + c - 3))
                    act.activation(w_hi[:, slot, :], raw[:, slot, :], ACT.Copy).then_inc(hi_ready, 1)

            def ahead(stage, first=0, extra=None):
                def body(i, k):
                    if FIRST[stage] + k + 1 < STEPS:
                        hi(i, FIRST[stage] + k + 1)
                    if extra is not None:
                        extra(i, k)
                steps(act, stage, body, first=first, last=2 if stage == "od_out" else 0)

            def squares(name, src, dst, wait):
                for q in range(4):
                    wait(q)
                    act.activation(dst[:, 4 * q:4 * q + 4, :], src[:, 4 * q:4 * q + 4, :], ACT.Square)\
                       .then_inc(S(f"{name}_sq"), 1)

            def root(name, buf):
                act.wait_ge(S(f"{name}_rs"), 1)
                act.activation(buf, buf, ACT.Sqrt).then_inc(S(f"{name}_rs"), 1)

            def shift_hi(name, y, dst, shift):
                for f in range(16):
                    act.wait_ge(S(f"{name}_y"), f + 1)
                    if shift is None:
                        ins = act.activation(dst[:, f, :], y[:, f, :], ACT.Copy)
                    else:
                        ins = act.activation(dst[:, f, :], y[:, f, :], ACT.Identity, bias=shift(f))
                    ins.then_inc(S(f"{name}_hi"), 1)

            def from_psum(name, dst):
                for g in range(0, 8, 2):
                    act.wait_ge(S(f"{name}_t"), g + 1)
                    act.activation(dst[:, 2 * g:2 * g + 2, :], ps[:, g, :], ACT.Copy).then_inc(S(f"{name}_fa"), 1)

            from_psum("x", res)
            squares("attn", res, sq, lambda q: (act.wait_ge(S("x_fa"), q + 1), act.wait_ge(S("x_fd"), q + 1)))
            hi(0, 0)
            act.wait_ge(S("const_in"), 32)
            act.activation(csil[:, :, :], col("cvec", 0, 32).rearrange("p (t c) -> p t c", c=2), ACT.Silu)\
               .then_inc(S("csil"), 1)
            root("attn", rstd[:, :])
            shift_hi("attn", sq, a_hi, None)
            ahead("conv", first=2)

            def conv_silu(i, k):
                if k % 2 == 0 and k < 28:
                    act.activation(pr[:, bass.ds(i, 1), :], pr[:, bass.ds(i, 1), :], ACT.Silu)
            act.wait_ge(dve_read, 16)
            ahead("rest", extra=conv_silu)
            act.activation(pr[:, 14:16, :], pr[:, 14:16, :], ACT.Silu).then_inc(S("g_silu"), 1)
            act.wait_ge(dve_read, dve_reads("out"))
            act.activation(pr[:, GOUT:GOUT + 8, :], pr[:, GOUT:GOUT + 8, :], ACT.Silu).then_inc(S("g_silu"), 1)

            act.wait_ge(S("g_z"), 1)
            for h in range(4):
                ins = act.activation(g_d[:, h, :], ps[:, 2 + h // 2, (h % 2) * T:(h % 2 + 1) * T], ACT.Abs,
                                     bias=col("gate_b", h))
            ins.then_inc(S("g_soft"), 1)
            act.wait_ge(S("g_soft"), 1)
            act.activation(g_d[:, :, :], g_d[:, :, :], ACT.Exp, scale=-1.0).then_inc(S("g_soft"), 1)
            act.wait_ge(S("g_soft"), 2)
            act.activation(g_d[:, :, :], g_d[:, :, :], ACT.Ln, bias=1.0).then_inc(S("g_soft"), 1)
            act.wait_ge(S("g_vt"), 1)
            for tt in range(TT):
                b0 = (0, 6)[tt]
                act.activation(v_tok[:, tt, :], ps[:, b0:b0 + 2, :].rearrange("p a n -> p (a n)"), ACT.Copy)\
                   .then_inc(S("g_vtok"), 1)
            for n in range(LEVELS + 1):
                act.wait_ge(S("g_diff"), 2 * (n + 1) if n < LEVELS else 2 * LEVELS + 1)
                act.activation(g_d[:, :, :], g_d[:, :, :], ACT.Exp, scale=1.0 / TAU).then_inc(S("g_dec"), 1)
            act.wait_ge(S("g_kdr"), 1)
            act.activation(g_d[:, :, :], g_b[:, :, :], ACT.Exp, scale=1.0 / TAU).then_inc(S("g_dec"), 1)
            act.activation(g_el[:, :, :], g_b[:, :, CHUNK - 1:T:CHUNK], ACT.Exp, scale=1.0 / TAU)\
               .then_inc(S("g_dec"), 1)
            act.wait_ge(S("g_kt"), 1)
            act.activation(k_tok[:, :, :], ps[:, 2:4, :], ACT.Copy).then_inc(S("g_ktok"), 1)
            for h in range(4):
                act.wait_ge(S("g_o"), h + 1)
                act.activation(g_sq[:, h, :, :], ps[:, (2, 3, 6, 7)[h], :].rearrange("p (e t) -> p e t", e=2),
                               ACT.Square).then_inc(S("g_sqr"), 1)
            act.wait_ge(S("g_rsr"), 1)
            act.activation(g_rs[:, :, :], g_rs[:, :, :], ACT.Sqrt).then_inc(S("g_rsr"), 1)
            act.wait_ge(S("g_yr"), 9)
            act.activation(b_hi[:, 0:8, :], g_y[:, :, :], ACT.Copy).then_inc(S("g_hi"), 1)

            act.wait_ge(S("g_out"), 1)
            act.activation(n_sq[:, :, :], pr[:, NQ:NQ + 12, :], ACT.Square).then_inc(S("n_sqr"), 1)
            act.wait_ge(S("n_gt"), 1)
            act.activation(gates[:, :, :], ps[:, 6, 0:64].rearrange("p (a b) -> p a b", a=2)[:, :, 0:24],
                           ACT.Sigmoid).then_inc(S("n_gs"), 1)
            act.wait_ge(side_used, 2 * CMP_HALVES)
            act.activation(hid[:, :].rearrange("p (a b) -> p a b", a=2),
                           ps[:, 7, 0:64].rearrange("p (a b) -> p a b", a=2)[:, :, 0:2 * N_CMP], ACT.Silu)\
               .then_inc(S("n_hs"), 1)
            act.wait_ge(S("n_kc"), 1)
            act.activation(c_sq[:, :], ps[:, 6, 0:2 * N_CMP], ACT.Square).then_inc(S("n_csq"), 1)
            act.wait_ge(S("n_msr"), 1)
            act.activation(n_rs[:, :, :], n_rs[:, :, :], ACT.Sqrt).then_inc(S("n_rt"), 1)
            act.wait_ge(S("n_crs"), 1)
            act.activation(c_rs[:, :], c_rs[:, :], ACT.Sqrt).then_inc(S("n_crt"), 1)
            act.wait_ge(S("n_vt"), 1)
            act.activation(v_nsa[:, :, :, :], ps[:, 0:2, :].rearrange("p a (f n) -> p a f n", f=4), ACT.Copy)\
               .then_inc(S("n_vtok"), 1)
            for tt in range(TT):
                act.wait_ge(S("c_sub"), tt + 1)
                act.activation(c_s[:, tt, :, :], c_s[:, tt, :, :], ACT.Exp).then_inc(S("c_exp"), 1)

            def attend(name):
                a = att(name)
                base = a["base"]
                for h in range(8):
                    act.wait_ge(S("at_nb_r"), base + h + 1)
                    src = ps[:, 2 + h % 4, :].rearrange("p (a n) -> p a n", a=2)
                    if a["kind"] == "n":
                        for part in range(2):
                            ins = act.activation(a["prob"][:, h, part, 0:a["keys"]], src[:, part, 0:a["keys"]],
                                                 ACT.Exp, bias=at_nb[:, 2 * h + part:2 * h + part + 1], scale=SCALE,
                                                 accum_out=at_den[:, 2 * h + part:2 * h + part + 1])
                    else:
                        ins = act.activation(a["prob"][:, h, :, :], src, ACT.Exp, bias=at_nb[:, h:h + 1],
                                             scale=SCALE, accum_out=at_den[:, h:h + 1])
                    ins.then_inc(S("at_exp"), 1)
                if a["kind"] == "b":
                    act.wait_ge(S("at_sd"), a["tt"] + 1)
                    act.activation(at_sink[:, :], at_sink[:, :], ACT.Exp).then_inc(S("at_se"), 1)
                for h in range(8):
                    act.wait_ge(S("at_t"), base + h + 1)
                    if h >= 2:
                        act.wait_ge(S("at_pv"), base + h - 1)
                    n = len(a["blocks"])
                    if a["kind"] == "n":
                        act.activation(a["prob_t"][0:N_CMP, h % 2, 4, :], ps[0:N_CMP, 2 + h % 2, 0:P], ACT.Copy)
                    act.activation(a["prob_t"][:, h % 2, 0:n, :],
                                   ps[:, h % 2, 0:n * P].rearrange("p (a n) -> p a n", n=P), ACT.Copy)\
                       .then_inc(S("at_pt"), 1)

            attend("n0")
            attend("n1")
            act.wait_ge(S("at_out"), 16)
            act.activation(b_hi[:, 8:16, :], pr[:, NQ:NQ + 8, :], ACT.Copy).then_inc(S("mix_hi"), 1)

            ahead("out")
            squares("ffn", res, sq, lambda q: act.wait_ge(dve_read, dve_reads("up0")))
            root("ffn", rstd[:, :])
            shift_hi("ffn", sq, a_hi, None)
            act.activation(sg[:, 1, 0:2], ident[:, 0:2], ACT.Copy).then_inc(silu_ready, 1)
            for c, n in enumerate(CHUNKS):
                ahead(f"up{c}", extra=gate_silu_steps(act, f"up{c}", sum(CHUNKS[:c])))
                ahead(f"down{c}")

            squares("ev", res, sq, lambda q: act.wait_ge(dve_read, dve_reads("ev_kv")))
            root("ev", rstd[:, :])
            shift_hi("ev", sq, a_hi, lambda f: mods[:, f, 0:1])
            act.wait_ge(S("ev_lo"), 16)
            from_psum("ctx", ctx_f)
            squares("ctx", ctx_f, sq2, lambda q: (act.wait_ge(S("ctx_fa"), q + 1), act.wait_ge(S("ctx_fd"), q + 1)))
            root("ctx", rstd[:, :])
            shift_hi("ctx", sq2, b_hi, lambda f: mods[:, f, 1:2])
            ahead("ev_kv")
            ahead("ev_q")
            act.wait_ge(dve_read, dve_reads("ev_z"))
            for dst, src in ((slice(0, 2), slice(0, 2)), (slice(2, 4), slice(8, 10)), (slice(4, 12), slice(16, 24))):
                act.activation(e_sq[:, dst, :], pr[:, src, :], ACT.Square).then_inc(S("e_sqr"), 1)
            act.wait_ge(S("e_msr"), 1)
            act.activation(e_rs[:, :, :], e_rs[:, :, :], ACT.Sqrt).then_inc(S("e_rt"), 1)
            act.wait_ge(S("e_vt"), 1)
            act.wait_ge(S("e_rope"), len(ROPE_PAIRS))
            for n in range(4):
                act.activation(v_ev[:, n // 2, n % 2, :, :], ps[:, 4 + n, :].rearrange("p (f n) -> p f n", f=4),
                               ACT.Copy).then_inc(S("e_vtok"), 1)
            for name in ("a0", "a1", "b0", "b1"):
                attend(name)
            ahead("ev_z", extra=z_silu_steps(act, "ev_z", 0))
            ahead("ev_out")
            squares("ev_post", pr, sq2, lambda q: act.wait_ge(dve_read, dve_reads("od_u")))
            root("ev_post", rstd[:, :])

            squares("od", res, sq, lambda q: act.wait_ge(S("ev_res"), 1))
            root("od", rstd[:, :])
            shift_hi("od", sq, a_hi, lambda f: mods[:, 48 + f, 0:1])
            ahead("od_u")
            for g in range(4):
                act.wait_ge(S("pool_y"), g + 1)
                act.activation(b_hi[:, 4 * g:4 * g + 4, :], pooled[:, 4 * g:4 * g + 4, :], ACT.Copy)\
                   .then_inc(S("pool_hi"), 1)
            for k in range(4):
                hi(0, FIRST["pool"] + k + 1)
            ahead("od_z", extra=z_silu_steps(act, "od_z", 16))
            ahead("od_out")
            squares("od_post", pr, sq2, lambda q: act.wait_ge(dve_read, dve_reads("od_out") + 16))
            root("od_post", rstd[:, :])
            for n in range(0, 8, 2):
                act.wait_ge(S("o_t"), n + 1)
                act.activation(o_tok[:, n // 4, (n % 4) * 512:(n % 4 + 1) * 512], ps[:, n, :], ACT.Copy)\
                   .then_inc(S(f"o_tok{n // 4}_a"), 1)

        @block.vector
        def _(dve):
            def lo(i, s):
                for c in range(2):
                    slot = 2 * (s % 2) + c
                    dve.wait_ge(hi_ready, i * 4 + (2 * s + c + 1))
                    dve.tensor_tensor(w_lo[:, slot, :], raw[:, slot, :], w_hi[:, slot, :].bitcast(F32), ALU.subtract)\
                       .then_inc(lo_ready, 1)

            def reading(stage, read, first=0):
                def body(i, k):
                    s = FIRST[stage] + k
                    if s + 1 < STEPS:
                        lo(i, s + 1)
                    dve.wait_ge(halves_used, i * 4 + (2 * s + 2))
                    read(i, k, s % 2)
                steps(dve, stage, body, first=first, last=2 if stage == "od_out" else 0)

            def tile(t, i, k):
                return t[:, k:k + 1, :] if isinstance(i, int) else t[:, bass.ds(i * 2 + k, 1), :]

            def psum_tile(bank):
                return ps[:, bank:bank + 1, 0:T]

            def mean_to_rstd(name, src, dst, width):
                dve.wait_ge(S(f"{name}_ms"), 1)
                dve.tensor_scalar(dst, src, 1.0 / width, EPS, ALU.mult, ALU.add).then_inc(S(f"{name}_rs"), 1)
                dve.wait_ge(S(f"{name}_rs"), 2)
                dve.reciprocal(dst, dst).then_inc(S(f"{name}_rs"), 1)
                dve.wait_ge(S(f"{name}_rs"), 3)

            def norm(name, src, y, gain, shift, hi_t, lo_t):
                mean_to_rstd(name, ps[:, 2, 0:T], rstd[:, :], D)
                for f in range(16):
                    dve.scalar_tensor_tensor(out=y[:, f, :], in0=src[:, f, :], scalar=gain(f), in1=rstd[:, :],
                                             op0=ALU.mult, op1=ALU.mult).then_inc(S(f"{name}_y"), 1)
                for f in range(16):
                    dve.wait_ge(S(f"{name}_hi"), f + 1)
                    h = hi_t[:, f, :].bitcast(F32)
                    if shift is None:
                        ins = dve.tensor_tensor(lo_t[:, f, :], y[:, f, :], h, ALU.subtract)
                    else:
                        ins = dve.scalar_tensor_tensor(out=lo_t[:, f, :], in0=y[:, f, :], scalar=shift(f), in1=h,
                                                       op0=ALU.add, op1=ALU.subtract)
                    ins.then_inc(S(f"{name}_lo"), 1)

            def post_norm(name, gate):
                mean_to_rstd(name, ps[:, 2, 0:T], rstd[:, :], D)
                for f in range(16):
                    ins = dve.scalar_tensor_tensor(out=sq2[:, f, :], in0=pr[:, f, :], scalar=gate[:, f:f + 1],
                                                   in1=rstd[:, :], op0=ALU.mult, op1=ALU.mult)
                ins.then_inc(S(f"{name}_y"), 1)
                dve.wait_ge(S(f"{name}_y"), 1)
                return dve.tensor_tensor(res[:, :, :], res[:, :, :], sq2[:, :, :], ALU.add)

            def from_psum(name, dst):
                for g in range(1, 8, 2):
                    dve.wait_ge(S(f"{name}_t"), g + 1)
                    dve.tensor_copy(dst[:, 2 * g:2 * g + 2, :], ps[:, g, :].rearrange("p (a t) -> p a t", a=2))\
                       .then_inc(S(f"{name}_fd"), 1)

            dve.wait_ge(S("const_in"), 32)
            from_psum("x", res)
            norm("attn", res, sq, lambda f: col("attn_g", f), None, a_hi, a_lo)
            lo(0, 0)
            conv = S("conv_tap")

            def conv_read(i, k, bank):
                u, y = ps[:, bank:bank + 1, 0:T], tile(pr, i, k)

                def w(tap):
                    a = COLS["conv"][0] + 16 * tap + k
                    return cols[:, a:a + 1] if isinstance(i, int) else cols[:, bass.ds(i * 2 + a, 1)]
                dve.tensor_scalar(y, u, w(3), None, ALU.mult).then_inc(conv, 1)
                for n in range(1, 4):
                    dve.wait_ge(conv, i * 6 + (3 * k + n))
                    ins = dve.scalar_tensor_tensor(out=y[:, :, n:T], in0=u[:, :, 0:T - n], scalar=w(3 - n),
                                                   in1=y[:, :, n:T], op0=ALU.mult, op1=ALU.add)
                    if n < 3:
                        ins.then_inc(conv, 1)
                ins.then_inc(dve_read, 1)

            reading("conv", conv_read, first=2)

            def copy_read(dst, k0=0):
                def read(i, k, bank):
                    dve.tensor_copy(tile(dst, i, k + k0), psum_tile(bank)).then_inc(dve_read, 1)
                return read

            reading("rest", copy_read(pr, 16))

            dve.memset(g_keep[:, :, :], 1.0).then_inc(S("g_v"), 1)
            dve.memset(g_q[:, :, :], 0.0)
            dve.memset(g_k[:, :, :], 0.0)
            dve.wait_ge(S("g_v"), 1)
            dve.memset(g_keep[:, :, 0:T:CHUNK], 0.0).then_inc(S("g_v"), 1)
            dve.wait_ge(S("g_soft"), 1)
            for h in range(4):
                ins = dve.tensor_scalar(g_kd[:, h, :], ps[:, 2 + h // 2, (h % 2) * T:(h % 2 + 1) * T],
                                        col("gate_b", h), 0.0, ALU.add, ALU.min)
            ins.then_inc(S("g_v"), 1)
            dve.wait_ge(S("g_v"), 3)
            dve.wait_ge(S("g_soft"), 3)
            dve.tensor_tensor(g_kd[:, :, :], g_kd[:, :, :], g_d[:, :, :], ALU.subtract).then_inc(S("g_v"), 1)
            dve.wait_ge(S("g_v"), 4)
            flat = "p a t -> p (a t)"
            dve.tensor_tensor_scan(g_b[:, :, :].rearrange(flat), g_keep[:, :, :].rearrange(flat),
                                   g_kd[:, :, :].rearrange(flat), 0.0, ALU.mult, ALU.add).then_inc(S("g_v"), 1)
            dve.wait_ge(S("g_v"), 5)

            def level_views(t, half):
                v = t.rearrange("p a t -> p (a t)").rearrange("p (n w) -> p n w", w=2 * half)
                return v[:, :, 0:half], v[:, :, half:2 * half]

            def level_diff(lv):
                half = 1 << lv
                b_first, b_second = level_views(g_b[:, :, :], half)
                d_first, d_second = level_views(g_d[:, :, :], half)
                mid = b_first[:, :, half - 1:half].to_broadcast([P, 4 * T // (2 * half), half])
                dve.tensor_tensor(d_first, mid, b_first, ALU.subtract).then_inc(S("g_diff"), 1)
                dve.tensor_tensor(d_second, b_second, mid, ALU.subtract).then_inc(S("g_diff"), 1)

            def level_mul(lv):
                half = 1 << lv
                dve.wait_ge(S("g_dec"), lv + 1)
                dve.wait_ge(S("g_s"), lv + 1)
                k1, _ = level_views(pr[:, KT:KT + 4, :], half)
                _, q2 = level_views(pr[:, QT:QT + 4, :], half)
                d1, d2 = level_views(g_d[:, :, :], half)
                dve.tensor_tensor(level_views(g_k[:, :, :], half)[0], k1, d1, ALU.mult).then_inc(S("g_mul"), 1)
                dve.tensor_tensor(level_views(g_q[:, :, :], half)[1], q2, d2, ALU.mult).then_inc(S("g_mul"), 1)
                dve.wait_ge(S("g_mul"), 2 * (lv + 1))

            def level_mask(n, m):
                dve.wait_ge(S("g_s"), n)
                dst = g_sc if n == 1 else g_tmp
                for tt in range(TT):
                    if n > 2:
                        dve.wait_ge(S("g_add"), 2 * (n - 2) - 1 + tt)
                    dve.tensor_tensor(dst[:, tt, :, :], ps[:, 4 + tt, :].rearrange("p (h t) -> p h t", h=4),
                                      cbc(table[:, m * P:(m + 1) * P], 4), ALU.mult).then_inc(S("g_msk"), 1)
                if n > 1:
                    for tt in range(TT):
                        dve.wait_ge(S("g_msk"), 2 * (n - 1) + tt + 1)
                        dve.tensor_tensor(g_sc[:, tt, :, :], g_sc[:, tt, :, :], g_tmp[:, tt, :, :], ALU.add)\
                           .then_inc(S("g_add"), 1)

            level_diff(0)
            level_mask(1, 6)
            for lv in range(LEVELS):
                level_mul(lv)
                if lv + 1 < LEVELS:
                    level_diff(lv + 1)
                else:
                    last = g_b[:, :, :].rearrange(flat).rearrange("p (n w) -> p n w", w=CHUNK)
                    dve.tensor_tensor(g_d[:, :, :].rearrange(flat).rearrange("p (n w) -> p n w", w=CHUNK),
                                      last[:, :, CHUNK - 1:CHUNK].to_broadcast([P, 16, CHUNK]), last, ALU.subtract)\
                       .then_inc(S("g_diff"), 1)
                level_mask(lv + 2, lv)
            dve.wait_ge(S("g_dec"), LEVELS + 1)
            dve.tensor_tensor(g_kd[:, :, :], pr[:, KT:KT + 4, :], g_d[:, :, :], ALU.mult).then_inc(S("g_kdr"), 1)
            dve.wait_ge(S("g_dec"), LEVELS + 2)
            dve.tensor_tensor(g_qe[:, :, :], pr[:, QT:QT + 4, :], g_d[:, :, :], ALU.mult)
            dve.wait_ge(S("g_kv"), 1)
            dve.wait_ge(S("g_dec"), LEVELS + 3)
            for c in range(3):
                bank = 2 * (c % 2)
                src = ps[:, bank:bank + 2, :].rearrange("p a n -> p (a n)")
                dve.wait_ge(S("g_kv"), c + 1)
                if c == 0:
                    ins = dve.tensor_copy(state[:, 0, :], src)
                else:
                    dve.wait_ge(S("g_state"), c)
                    for h in range(4):
                        part = slice(h * 256, (h + 1) * 256)
                        ins = dve.scalar_tensor_tensor(out=state[:, c, part], in0=state[:, c - 1, part],
                                                       scalar=g_el[:, h, c:c + 1], in1=src[:, part],
                                                       op0=ALU.mult, op1=ALU.add)
                ins.then_inc(S("g_state"), 1)
            dve.wait_ge(S("g_ms"), 1)
            dve.tensor_scalar(g_rs[:, :, :].rearrange(flat), ps[:, 4:6, :].rearrange("p a n -> p (a n)"),
                              1.0 / GLA_DV, EPS * DH, ALU.mult, ALU.add).then_inc(S("g_rsr"), 1)
            dve.wait_ge(S("g_rsr"), 2)
            dve.reciprocal(g_rs[:, :, :], g_rs[:, :, :]).then_inc(S("g_rsr"), 1)
            dve.wait_ge(S("g_rsr"), 3)
            for h in range(4):
                for e in range(2):
                    dve.scalar_tensor_tensor(out=g_y[:, 2 * h + e, :], in0=ps[:, (2, 3, 6, 7)[h], e * T:(e + 1) * T],
                                             scalar=col("gla_g", e), in1=g_rs[:, h, :], op0=ALU.mult, op1=ALU.mult)\
                       .then_inc(S("g_yr"), 1)
            dve.wait_ge(S("g_yr"), 8)
            dve.wait_ge(S("g_silu"), 2)
            dve.tensor_tensor(g_y[:, :, :], g_y[:, :, :], pr[:, GOUT:GOUT + 8, :], ALU.mult).then_inc(S("g_yr"), 1)
            dve.wait_ge(S("g_hi"), 1)
            dve.wait_ge(S("g_yr"), 9)
            dve.tensor_tensor(b_lo[:, 0:8, :], g_y[:, :, :], b_hi[:, 0:8, :].bitcast(F32), ALU.subtract)\
               .then_inc(S("g_out"), 1)
            dve.wait_ge(S("g_out"), 1)

            for kv in range(2):
                src_t, pos = ((NKC, "k_pos"), (NVC, "v_pos"))[kv]
                for g in range(2):
                    base = pr[:, src_t + g, :]
                    for part in range(2):
                        v = base[:, 16 * part:16 * part + 16 * N_CMP].rearrange("p (n j) -> p j n", j=16)
                        dst = n_x[:, kv, 16 * part:16 * part + 16, g * N_CMP:(g + 1) * N_CMP]
                        ins = dve.tensor_tensor(dst, v, vbc(col(pos, 16 * part, 16), N_CMP), ALU.add)
                ins.then_inc(S("n_xr"), 1)
            dve.wait_ge(S("n_ms"), 1)
            dve.tensor_scalar(n_rs[:, :, :].rearrange(flat), ps[:, 0:6, :].rearrange("p a n -> p (a n)"),
                              1.0 / DH, EPS, ALU.mult, ALU.add).then_inc(S("n_msr"), 1)
            dve.wait_ge(S("n_rt"), 1)
            dve.reciprocal(n_rs[:, :, :], n_rs[:, :, :]).then_inc(S("n_rr"), 1)
            dve.wait_ge(S("n_rr"), 1)
            for t0, n, g in ((NQ, 8, "q_g"), (NKS, 2, "ks_g"), (NKW, 2, "kw_g")):
                dve.scalar_tensor_tensor(out=pr[:, t0:t0 + n, :], in0=pr[:, t0:t0 + n, :], scalar=col(g),
                                         in1=n_rs[:, t0 - NQ:t0 - NQ + n, :], op0=ALU.mult, op1=ALU.mult)\
                   .then_inc(S("n_qk"), 1)
            dve.wait_ge(S("n_vc"), 1)
            dve.tensor_copy(v_cmp[:, :, :], ps[0:N_CMP, 7, 0:2 * P].rearrange("p (a n) -> p a n", a=2))
            dve.wait_ge(S("n_cms"), 1)
            dve.tensor_scalar(c_rs[:, :], ps[:, 2, 0:2 * N_CMP], 1.0 / DH, EPS, ALU.mult, ALU.add)\
               .then_inc(S("n_crs"), 1)
            dve.wait_ge(S("n_crt"), 1)
            dve.reciprocal(c_rs[:, :], c_rs[:, :]).then_inc(S("n_crs"), 1)
            dve.wait_ge(S("n_crs"), 2)
            dve.scalar_tensor_tensor(out=k_cmp[:, :], in0=ps[:, 6, 0:2 * N_CMP], scalar=col("kc_g"),
                                     in1=c_rs[:, :], op0=ALU.mult, op1=ALU.mult).then_inc(S("n_kcn"), 1)
            dve.wait_ge(S("n_cs"), 1)
            dve.wait_ge(S("n_gs"), 1)
            add_a, ok_a = CONS["cmp_add"][0], CONS["cmp_ok"][0]
            link = S("c_link")
            links = [0]

            def then(ins):
                links[0] += 1
                ins.then_inc(link, 1)
                dve.wait_ge(link, links[0])

            for tt in range(TT):
                cs, mx, den = c_s[:, tt, :, :], c_mx[:, tt, :], c_den[:, tt, :]
                sc = ps[:, 2 + tt, 0:P].rearrange("p (h n) -> p h n", h=8)[:, :, 0:N_CMP]
                add = cons[:, add_a + tt * N_CMP:add_a + (tt + 1) * N_CMP]
                then(dve.scalar_tensor_tensor(out=cs, in0=sc, scalar=SCALE, in1=cbc(add, 8), op0=ALU.mult, op1=ALU.add))
                then(dve.tensor_reduce(mx, cs, AX.X, ALU.max))
                dve.tensor_tensor(cs, cs, vbc(mx, N_CMP), ALU.subtract).then_inc(S("c_sub"), 1)
            for tt in range(TT):
                cs, mx, den = c_s[:, tt, :, :], c_mx[:, tt, :], c_den[:, tt, :]
                ok = cons[:, ok_a + tt * N_CMP:ok_a + (tt + 1) * N_CMP]
                dve.wait_ge(S("c_exp"), tt + 1)
                then(dve.tensor_reduce(den, cs, AX.X, ALU.add))
                then(dve.reciprocal(den, den))
                then(dve.tensor_tensor(den, den, gates[:, tt, 0:24:3], ALU.mult))
                then(dve.tensor_tensor(cs, cs, cbc(ok, 8), ALU.mult))
                dve.tensor_tensor(c_p[:, tt, :, :], cs, vbc(den, N_CMP), ALU.mult).then_inc(S("c_ready"), 1)

            def attend(name):
                a = att(name)
                base, tt, kind = a["base"], a["tt"], a["kind"]
                for h in range(8):
                    bank = 2 + h % 4
                    dve.wait_ge(S("at_sc"), base + h + 1)
                    for part, b, m in a["mask"]:
                        blk = ps[:, bank, part * T + b * P:part * T + (b + 1) * P]
                        last = dve.tensor_tensor(blk, blk, con(m), ALU.add)
                    if a["mask"]:
                        then(last)
                    if kind == "n":
                        src = ps[:, bank, :].rearrange("p (a n) -> p a n", a=2)[:, :, 0:a["keys"]]
                        mx, nb = at_max[:, 2 * h:2 * h + 2], at_nb[:, 2 * h:2 * h + 2]
                    else:
                        src, mx, nb = ps[:, bank, :], at_max[:, h:h + 1], at_nb[:, h:h + 1]
                    then(dve.tensor_reduce(mx, src, AX.X, ALU.max))
                    if kind == "b":
                        ins = dve.tensor_scalar(nb, mx, -SCALE, neg_sink[:, h:h + 1], ALU.mult, ALU.min)
                    else:
                        ins = dve.tensor_scalar(nb, mx, -SCALE, None, ALU.mult)
                    ins.then_inc(S("at_nb_r"), 1)
                n = 16 if kind == "n" else 8
                if kind == "b":
                    dve.wait_ge(S("at_nb_r"), base + 8)
                    dve.tensor_tensor(at_sink[:, :], at_nb[:, 0:8], col("sink", 0, 8), ALU.add).then_inc(S("at_sd"), 1)
                dve.wait_ge(S("at_exp"), base + 8)
                if kind == "b":
                    dve.wait_ge(S("at_se"), tt + 1)
                    then(dve.tensor_tensor(at_den[:, 0:8], at_den[:, 0:8], at_sink[:, :], ALU.add))
                then(dve.reciprocal(at_coef[:, 0:n], at_den[:, 0:n]))
                if kind == "n":
                    g = gates[:, tt, :].rearrange("p (h c) -> p h c", c=3)[:, :, 1:3]
                    then(dve.tensor_tensor(at_coef[:, :].rearrange("p (h c) -> p h c", c=2),
                                           at_coef[:, :].rearrange("p (h c) -> p h c", c=2), g, ALU.mult))

                def scale(h):
                    if kind == "n":
                        for part in range(2):
                            p_ap = a["prob"][:, h, part, 0:a["keys"]]
                            ins = dve.tensor_scalar(p_ap, p_ap, at_coef[:, 2 * h + part:2 * h + part + 1], None, ALU.mult)
                    else:
                        p_ap = a["prob"][:, h, :, :]
                        ins = dve.tensor_scalar(p_ap, p_ap, at_coef[:, h:h + 1], None, ALU.mult)
                    ins.then_inc(S("at_scl"), 1)

                def read(h):
                    dve.wait_ge(S("at_pv"), base + h + 1)
                    dve.tensor_copy(pr[:, a["q"](h), a["cols"]], ps[:, 6 + h % 2, 0:P]).then_inc(S("at_out"), 1)

                scale(0)
                scale(1)
                for h in range(8):
                    if h + 2 < 8:
                        scale(h + 2)
                    read(h)

            attend("n0")
            attend("n1")
            dve.wait_ge(S("mix_hi"), 1)
            dve.wait_ge(S("at_out"), 16)
            dve.tensor_tensor(b_lo[:, 8:16, :], pr[:, NQ:NQ + 8, :], b_hi[:, 8:16, :].bitcast(F32), ALU.subtract)\
               .then_inc(S("mix_lo"), 1)

            def add_res(i, k, bank):
                dve.tensor_tensor(tile(res, i, k), psum_tile(bank), tile(res, i, k), ALU.add).then_inc(dve_read, 1)

            reading("out", add_res)

            norm("ffn", res, sq, lambda f: col("ffn_g", f), None, a_hi, a_lo)
            dve.memset(gated[:, 0, :], 0.0).then_inc(S("gate_y"), 1)
            gate_hi = S("gate_hi")

            def split_out(i, per, n, other, dst_k, counted=True):
                y = gated[:, dst_k % per:dst_k % per + 1, :]
                dve.wait_ge(silu_ready, i * per + (n + 2))
                dve.tensor_tensor(y, other, sg[:, 0:1, :], ALU.mult).then_inc(S("gate_y"), 1)
                dve.wait_ge(S("gate_y"), i * per + (n + 2))
                bh = b_hi[:, dst_k:dst_k + 1, :] if isinstance(i, int) else b_hi[:, bass.ds(i * per + dst_k, 1), :]
                bl = b_lo[:, dst_k:dst_k + 1, :] if isinstance(i, int) else b_lo[:, bass.ds(i * per + dst_k, 1), :]
                dve.tensor_copy(bh, y).then_inc(gate_hi, 1)
                dve.wait_ge(gate_hi, i * per + (n + 1))
                dve.tensor_tensor(bl, y, bh.bitcast(F32), ALU.subtract).then_inc(S("gate_lo"), 1)

            for c, n in enumerate(CHUNKS):
                done = sum(CHUNKS[:c])

                def up_read(i, k, bank, done=done):
                    if k % 2:
                        split_out(i, 1, done + k // 2, psum_tile(bank), k // 2)
                reading(f"up{c}", up_read)
                reading(f"down{c}", add_res)

            dve.wait_ge(side_used, SIDE_HALVES)
            then(dve.tensor_tensor(mods[:, :, :], ps[:, 7, 0:2 * MOD_TILES].rearrange("p (m c) -> p m c", c=2),
                                   vbc(col("mod_b", 0, MOD_TILES), 2), ALU.add))
            for c in range(2):
                dve.scalar_tensor_tensor(out=ev_gain[:, :, c], in0=mods[:, 16:32, c], scalar=1.0,
                                         in1=col("ev_pre", 0, 16), op0=ALU.add, op1=ALU.mult)
            dve.scalar_tensor_tensor(out=od_gain[:, :], in0=mods[:, 64:80, 0], scalar=1.0,
                                     in1=col("od_pre", 0, 16), op0=ALU.add, op1=ALU.mult)
            dve.tensor_tensor(ev_gate[:, :], mods[:, 32:48, 0], col("ev_post", 0, 16), ALU.mult)
            dve.tensor_scalar(neg_sink[:, :], col("sink", 0, 8), -1.0, None, ALU.mult)
            dve.tensor_tensor(od_gate[:, :], mods[:, 80:96, 0], col("od_post", 0, 16), ALU.mult)\
               .then_inc(S("mods_read"), 1)
            dve.wait_ge(S("mods_read"), 1)

            norm("ev", res, sq, lambda f: ev_gain[:, f, 0:1], lambda f: mods[:, f, 0:1], a_hi, a_lo)
            dve.wait_ge(S("ev_lo"), 16)
            from_psum("ctx", ctx_f)
            norm("ctx", ctx_f, sq2, lambda f: ev_gain[:, f, 1:2], lambda f: mods[:, f, 1:2], b_hi, b_lo)

            def kv_read(i, k, bank):
                dve.tensor_copy(tile(pr, i, k), psum_tile(bank))
                dve.tensor_copy(tile(pr, i, k + 8), psum_tile(2 + bank)).then_inc(dve_read, 1)

            reading("ev_kv", kv_read)
            reading("ev_q", copy_read(pr, 16))
            dve.wait_ge(S("e_ms"), 1)
            dve.tensor_scalar(e_rs[:, :, :].rearrange(flat), ps[:, 2:8, :].rearrange("p a n -> p (a n)"),
                              1.0 / DH, EPS, ALU.mult, ALU.add).then_inc(S("e_msr"), 1)
            dve.wait_ge(S("e_rt"), 1)
            then(dve.reciprocal(e_rs[:, :, :], e_rs[:, :, :]))
            for t0, n, r0, g in ((0, 2, 0, "ev_kn"), (8, 2, 2, "ev_kn"), (16, 8, 4, "ev_qn")):
                dve.scalar_tensor_tensor(out=pr[:, t0:t0 + n, :], in0=pr[:, t0:t0 + n, :], scalar=col(g),
                                         in1=e_rs[:, r0:r0 + n, :], op0=ALU.mult, op1=ALU.mult)\
                   .then_inc(S("e_nrm"), 1)
            dve.wait_ge(S("e_nrm"), 3)
            for n, t0 in enumerate(ROPE_PAIRS):
                pair, tmp = pr[:, t0:t0 + 2, :], e_rot[:, n % 2, :, :]
                dve.wait_ge(S("e_rp"), n + 1)
                dve.tensor_tensor(tmp, ps[:, n % 4, :].rearrange("p (a t) -> p a t", a=2), cbc(con("sin"), 2),
                                  ALU.mult).then_inc(S("e_rot"), 1)
                then(dve.tensor_tensor(pair, pair, cbc(con("cos"), 2), ALU.mult))
                dve.tensor_tensor(pair, pair, tmp, ALU.add).then_inc(S("e_rope"), 1)
                dve.wait_ge(S("e_rope"), n + 1)
            for name in ("a0", "a1", "b0", "b1"):
                attend(name)
            dve.wait_ge(S("at_out"), 48)

            def z_read(done, k0):
                def read(i, k, bank):
                    other = tile(pr, i, k + k0)
                    split_out(i, 2, FFN_TILES + done + k, other, k)
                return read

            reading("ev_z", z_read(0, 16))
            reading("ev_out", copy_read(pr))
            post_norm("ev_post", ev_gate).then_inc(S("ev_res"), 1)
            dve.wait_ge(S("ev_res"), 1)

            norm("od", res, sq, lambda f: od_gain[:, f:f + 1], lambda f: mods[:, 48 + f, 0:1], a_hi, a_lo)
            reading("od_u", copy_read(pr))
            dve.wait_ge(dve_read, dve_reads("pool"))
            dve.wait_ge(S("counts_in"), 16)
            W = T + 8
            for g in range(4):
                u = pr[:, 4 * g:4 * g + 4, :]
                a_buf, b_buf = f_a, f_b
                dve.memset(a_buf[:, :, T:W], 0.0)
                then(dve.tensor_copy(a_buf[:, :, 0:T], u))
                for lv in range(g + 1):
                    w = 1 << lv
                    dve.tensor_copy(b_buf[:, :, 0:w], a_buf[:, :, 0:w])
                    then(dve.tensor_tensor(b_buf[:, :, w:W], a_buf[:, :, w:W], a_buf[:, :, 0:W - w], ALU.add))
                    a_buf, b_buf = b_buf, a_buf
                lag = (1 << g) - 1
                y = pooled[:, 4 * g:4 * g + 4, :]
                then(dve.tensor_tensor(y, a_buf[:, :, lag:lag + T], cbc(table[:, g * T:(g + 1) * T], 4), ALU.mult))
                dve.tensor_tensor(y, y, u, ALU.subtract).then_inc(S("pool_y"), 1)
            for g in range(4):
                dve.wait_ge(S("pool_hi"), g + 1)
                dve.tensor_tensor(b_lo[:, 4 * g:4 * g + 4, :], pooled[:, 4 * g:4 * g + 4, :],
                                  b_hi[:, 4 * g:4 * g + 4, :].bitcast(F32), ALU.subtract).then_inc(S("pool_lo"), 1)
            for g in range(4):
                s = FIRST["pool"] + g
                lo(0, s + 1)
                dve.wait_ge(halves_used, 2 * s + 2)
                for n in range(4):
                    ins = dve.tensor_scalar(pr[:, 4 * g + n, :], ps[:, 2 * (s % 2) + n // 2, (n % 2) * T:(n % 2 + 1) * T],
                                            col("pool_s", 4 * g + n), None, ALU.mult)
                ins.then_inc(dve_read, 1)
            dve.wait_ge(dve_read, dve_reads("od_z"))
            reading("od_z", z_read(16, 0))
            reading("od_out", copy_read(pr))
            post_norm("od_post", od_gate).then_inc(S("final"), 1)
            for n in range(1, 8, 2):
                dve.wait_ge(S("o_t"), n + 1)
                dve.tensor_copy(o_tok[:, n // 4, (n % 4) * 512:(n % 4 + 1) * 512], ps[:, n, :])\
                   .then_inc(S(f"o_tok{n // 4}_d"), 1)


def _tiles(w):
    k, n = w.shape
    kp = -(-k // 1024) * 1024
    if kp != k:
        w = np.concatenate([w, np.zeros((kp - k, n), w.dtype)])
    w = w.reshape(kp // 1024, 8, P, n // P, P)
    return w.transpose(3, 0, 2, 1, 4).reshape(-1, P, HALF)


def _column(v):
    v = np.asarray(v).reshape(-1)
    return v.reshape(-1, P).T


def _shape_constants():
    t = np.arange(T)
    ident = np.eye(P, dtype=np.float32)
    i, j = np.arange(P)[:, None], np.arange(P)[None, :]
    above = np.where(j > i, NEG, 0.0)
    below = np.where(j < i, NEG, 0.0)
    rot = np.zeros((P, P))
    rot[np.arange(64) + 64, np.arange(64)] = -1.0
    rot[np.arange(64), np.arange(64) + 64] = 1.0
    inv = (np.float32(10000.0) ** (-np.arange(32, dtype=np.float32) / np.float32(32))).astype(np.float32)
    row, colm = (t // 64).astype(np.float32), (t % 64).astype(np.float32)
    ang = np.concatenate([row[:, None] * inv, colm[:, None] * inv], axis=-1).astype(np.float32)
    cos, sin = np.cos(ang).T, np.sin(ang).T
    cos, sin = np.concatenate([cos, cos]), np.concatenate([sin, sin])
    end = np.arange(N_CMP) * CMP_STRIDE + CMP_W - 1
    ok = (end[None, :] <= t[:, None]).reshape(TT, P, N_CMP).transpose(1, 0, 2).reshape(P, -1)
    cons = np.concatenate([ident, np.ones((P, P)), above, below, rot, cos, sin,
                           np.where(ok, 0.0, NEG), ok.astype(np.float32)], axis=1).astype(np.float32)
    masks = []
    for lv in range(LEVELS):
        h = 1 << lv
        masks.append((i // (2 * h) == j // (2 * h)) & (i % (2 * h) < h) & (j % (2 * h) >= h))
    masks.append(i == j)
    masks = np.concatenate(masks, axis=1).astype(np.float32)
    counts = []
    for w in (2, 4, 8, 16):
        n = np.clip(t + w // 2, 0, T) - np.clip(t - w // 2, 0, T)
        counts.append(np.broadcast_to((1.0 / n).astype(np.float32), (P, T)))
    return cons, masks, np.concatenate(counts, axis=1)


def _pack(a):
    w = np.asarray(a["w_in"])[0]
    gla = w[:, 0:2048]
    lr = w[:, 2048:2064]
    gout = w[:, 2064:3088]
    nq = w[:, 3088:4112]
    kc, vc, ks, vs, kw, vw = (w[:, 4112 + 256 * n:4112 + 256 * (n + 1)] for n in range(6))
    ng = w[:, 5648:5672]
    z = np.zeros
    last = np.concatenate([lr, z((D, GATE_ROW - 16), w.dtype), ng, z((D, P - GATE_ROW - 24), w.dtype)], axis=1)
    parts = [_tiles(np.concatenate([gla, gout, nq, ks, kw, kc, vc, vs, vw, last], axis=1)),
             _tiles(np.asarray(a["w_out"])[0])]
    wg, wu, wd = (np.asarray(a[n])[0] for n in ("w_gate", "w_up", "w_down"))
    at = 0
    for n in CHUNKS:
        f = slice(at * P, (at + n) * P)
        g, u = _tiles(wg[:, f]), _tiles(wu[:, f])
        parts.append(np.stack([g.reshape(n, 2, P, HALF), u.reshape(n, 2, P, HALF)], axis=1).reshape(-1, P, HALF))
        parts.append(_tiles(wd[f]))
        at += n
    ev = np.asarray(a["ev_w_in_2"])[0]
    parts += [_tiles(ev[:, 2048:3072]), _tiles(ev[:, 0:2048]), _tiles(ev[:, 3072:]), _tiles(np.asarray(a["ev_w_out_2"])[0])]
    od = np.asarray(a["od_w_in_2"])[0]
    pool = np.asarray(a["od_pool_w_2"])[0].reshape(4, 4, P, 2, 2, P)
    parts += [_tiles(od[:, 0:2048]), pool.transpose(0, 3, 2, 4, 1, 5).reshape(-1, P, HALF),
              _tiles(od[:, 2048:]), _tiles(np.asarray(a["od_w_out_2"])[0])]
    w_main = np.concatenate(parts)
    assert w_main.shape[0] == HALVES
    w_side = np.concatenate([_tiles(np.asarray(a["cmp_k_w1"])[0]), _tiles(np.asarray(a["cmp_v_w1"])[0]),
                             _tiles(np.asarray(a["ev_mod_w_2"])[0]), _tiles(np.asarray(a["od_mod_w_2"])[0])])
    assert w_side.shape[0] == SIDE_HALVES
    cvec = np.stack([_column(a["c_2"]), _column(a["c_ctx_2"])], axis=2).reshape(P, 32)
    vectors = {
        "attn_g": _column(a["attn_norm_g"]), "conv": _column(a["gla_conv_w"]), "gate_b": _column(a["gla_gate_b"]),
        "gla_g": _column(a["gla_norm_g"]), "q_g": _column(a["nsa_q_norm_g"]), "kc_g": _column(a["nsa_kc_norm_g"]),
        "ks_g": _column(a["nsa_ks_norm_g"]), "kw_g": _column(a["nsa_kw_norm_g"]), "k_pos": _column(a["cmp_k_pos"]),
        "v_pos": _column(a["cmp_v_pos"]), "ffn_g": _column(a["ffn_norm_g"]), "ev_pre": _column(a["ev_pre_g_2"]),
        "ev_post": _column(a["ev_post_g_2"]), "od_pre": _column(a["od_pre_g_2"]), "od_post": _column(a["od_post_g_2"]),
        "pool_s": _column(a["od_pool_scale_2"]),
        "mod_b": np.concatenate([_column(a["ev_mod_b_2"]), _column(a["od_mod_b_2"])], axis=1),
        "cvec": cvec, "ev_qn": _column(a["ev_q_norm_2"]), "ev_kn": _column(a["ev_k_norm_2"]),
        "sink": np.broadcast_to(np.asarray(a["ev_sink_2"]).reshape(1, 8), (P, 8)),
    }
    cols = np.concatenate([vectors[n] for n in COLS], axis=1)
    assert cols.shape == (P, NCOLS)
    cons, masks, counts = _shape_constants()
    cmp_w2 = np.stack([np.asarray(a["cmp_k_w2"])[0], np.asarray(a["cmp_v_w2"])[0]], axis=1)
    return {
        "x_in": np.asarray(a["x"])[0], "ctx_tok": np.asarray(a["ctx_2"])[0], "w_main": w_main, "w_side": w_side,
        "cols_in": cols, "cons_in": cons, "masks_in": masks, "counts_tab": counts,
        "gate_w2_in": np.asarray(a["gla_gate_w2"])[0], "cmp_w2_in": cmp_w2,
    }


def kernel(**inputs):
    import concourse.bacc as _bacc
    from concourse.bass_utils import run_bass_kernel_spmd as _run

    nc = _bacc.Bacc("TRN2", target_bir_lowering=False, num_devices=1)
    arrays = {name: np.ascontiguousarray(a) for name, a in _pack(inputs).items()}
    args = [nc.dram_tensor(name, a.shape, mybir.dt.from_np(a.dtype), kind="ExternalInput").ap()
            for name, a in arrays.items()]
    args.append(nc.dram_tensor("y_out", (T, D), F32, kind="ExternalOutput").ap())
    build(nc, *args)
    r = _run(nc, [arrays], core_ids=[0])
    return r.results[0]["y_out"].reshape(1, T, D)
```

```python
from contextlib import ExitStack

import numpy as np
import concourse.bass as bass
from concourse import mybir

F32 = mybir.dt.float32
F32R = mybir.dt.float32r
ACT = mybir.ActivationFunctionType
ALU = mybir.AluOpType
AX = mybir.AxisListType

P = 128
T = 256
TT = T // P
D = 2048
DT = D // P
EPS = 1e-6
NEG = -1e30
HALF = 8 * P
DH = 128
GLA_H, GLA_DV = 4, 256
CHUNK, TAU = 64, 16.0
NSA_H, CMP_W, CMP_STRIDE = 8, 32, 16
N_CMP = (T - CMP_W) // CMP_STRIDE + 1
FFN_TILES = 5632 // P
CHUNKS = (16, 16, 12)
assert sum(CHUNKS) == FFN_TILES
SCALE = DH ** -0.5

QT, KT, VT, GOUT = 0, 4, 8, 16
NQ, NKS, NKW, NKC, NVC, NVS, NVW, LAST = 24, 32, 34, 36, 38, 40, 42, 44
GATE_ROW = 32

STAGES = [("conv", 16), ("rest", 29), ("out", 16),
          ("up0", 32), ("down0", 16), ("up1", 32), ("down1", 16), ("up2", 24), ("down2", 16),
          ("ev_kv", 8), ("ev_q", 16), ("ev_z", 16), ("ev_out", 16),
          ("od_u", 16), ("pool", 4), ("od_z", 16), ("od_out", 16)]
FIRST, COUNT = {}, {}
_s = 0
for _n, _c in STAGES:
    FIRST[_n], COUNT[_n] = _s, _c
    _s += _c
STEPS = _s
HALVES = 2 * STEPS
CMP_HALVES = 4
MOD_TILES = 96
MOD_GROUPS = {"conv": 4, "rest": 0, "out": 1, "up0": 2, "down0": 3, "up1": 5,
              "down1": 6, "up2": 7, "down2": 8, "ev_q": 9, "ev_z": 10, "ev_out": 11}
MOD_STAGES = list(MOD_GROUPS)
assert len(MOD_STAGES) == MOD_TILES // 8 and all(COUNT[n] >= DT for n in MOD_STAGES)
BOTH = (0, 1, 2, 3)
CMP_AT = 2 * DT
SIDE_HALVES = 2 * CMP_HALVES + 2 * MOD_TILES


def mod_half(stage, k):
    m = DT * MOD_STAGES.index(stage) + k
    return m + (2 * CMP_HALVES if m >= CMP_AT else 0), m


COLS = {}
_o = 0
for _n, _w in [("attn_g", 16), ("conv", 64), ("gate_b", 4), ("gla_g", 2), ("q_g", 1), ("kc_g", 1),
               ("ks_g", 1), ("kw_g", 1), ("k_pos", 32), ("v_pos", 32), ("ffn_g", 16), ("ev_pre", 16),
               ("ev_post", 16), ("od_pre", 16), ("od_post", 16), ("pool_s", 16), ("mod_b", 96),
               ("cvec", 32), ("ev_qn", 1), ("ev_kn", 1), ("sink", 8)]:
    COLS[_n] = (_o, _w)
    _o += _w
NCOLS = _o

CONS = {}
_o = 0
for _n, _w in [("ident", P), ("ones", P), ("above", P), ("below", P), ("rot", P), ("cos", T), ("sin", T),
               ("cmp_add", TT * N_CMP), ("cmp_ok", TT * N_CMP)]:
    CONS[_n] = (_o, _w)
    _o += _w
NCONS = _o
O_BANKS = (2, 3, 6, 1)
LEVELS = 6
TABLE = 4 * T


def steps(eng, stage, body, first=0, last=0, splits=(), between=None):
    n = COUNT[stage]
    for k in range(first):
        body(0, k)
    cuts = [first] + [k for k in splits if first < k < n - last] + [n - last]
    for k0, k1 in zip(cuts, cuts[1:]):
        if between is not None and k0 > first:
            between(k0)
        pairs = (k1 - k0) // 2
        with eng.Fori(0, pairs) as i:
            body(i, k0)
            body(i, k0 + 1)
        for k in range(k0 + 2 * pairs, k1):
            body(0, k)
    for k in range(n - last, n):
        body(0, k)


def dve_reads(stage):
    n = 0
    for name, count in STAGES:
        if name == stage:
            return n
        n += 0 if name[:2] == "up" or name[-2:] == "_z" else count


ROPE_PAIRS = [0, 4] + list(range(16, 32, 2))
ROPE_BANKS, V_BANKS = (2, 3, 6), (4, 5, 0, 1)


def build(nc, x, ctx_in, w_main, w_side, cols_in, cons_in, gla_masks_in, counts_in, gate_w2_in, cmp_w2_in, out):
    stack = ExitStack()
    with stack:
        K = 1024
        sems = {}

        def S(name):
            if name not in sems:
                sems[name] = stack.enter_context(nc.semaphore(name))
            return sems[name]

        start = -(-nc.sbuf_base // 64) * 64

        def at(name, offset, shape, dtype=F32):
            return nc.alloc_sbuf_tensor_at(name, shape, dtype, offset=start + offset)

        RAW, HI, LO, SIDE, RES, A, B, PR, CO = (0, 16 * K, 32 * K, 48 * K, 64 * K, 80 * K, 112 * K, 144 * K, 189 * K)
        raw = at("raw", RAW, [P, 4, HALF])
        w_hi = at("w_hi", HI, [P, 4, HALF], F32R)
        w_lo = at("w_lo", LO, [P, 4, HALF], F32R)
        side = at("side", SIDE, [P, 2, HALF])
        mod_sum = at("mod_sum", SIDE + 8 * K, [P, 2, HALF])
        res = at("res", RES, [P, DT, T])
        a_hi = at("a_hi", A, [P, 16, T], F32R)
        a_lo = at("a_lo", A + 16 * K, [P, 16, T], F32R)
        b_hi = at("b_hi", B, [P, 16, T], F32R)
        b_lo = at("b_lo", B + 16 * K, [P, 16, T], F32R)
        pr = at("pr", PR, [P, 45, T])
        place = [CO]

        def small(name, shape):
            n = 4
            for d in shape[1:]:
                n *= d
            place[0] += -(-n // 32) * 32
            return at(name, place[0] - -(-n // 32) * 32, shape)

        cons = small("cons", [P, NCONS])
        cols = small("cols", [P, NCOLS])
        table = small("table", [P, TABLE])
        gate_w2 = small("gate_w2", [P, 512])
        cmp_w2 = small("cmp_w2", [P, 2, P])
        rstd = small("rstd", [P, T])
        csil = small("csil", [P, 16, 2])
        mods = small("mods", [P, MOD_TILES, 2])
        ev_gain = small("ev_gain", [P, 16, 2])
        od_gain = small("od_gain", [P, 16])
        ev_gate = small("ev_gate", [P, 16])
        od_gate = small("od_gate", [P, 16])
        neg_sink = small("neg_sink", [P, 8])
        at_max = small("at_max", [P, 16])
        at_nb = small("at_nb", [P, 16])
        at_den = small("at_den", [P, 16])
        at_coef = small("at_coef", [P, 16])
        at_sink = small("at_sink", [P, 8])
        q_rs = small("q_rs", [P, TT, 8])
        q_nrs = small("q_nrs", [P, TT, 8])
        kq_g = small("kq_g", [P, 2])
        rot_g = small("rot_g", [P, 1, P])
        x_tok = at("x_tok", B, [P, TT, D])
        sq = at("sq", PR, [P, 16, T])
        sq2 = at("sq2", PR + 16 * K, [P, 16, T])
        ctx_f = at("ctx_f", PR, [P, DT, T])
        ctx_tok = at("ctx_tok", PR + 16 * K, [P, TT, D])
        g_b = at("g_b", A, [P, 4, T])
        g_d = at("g_d", A + 4 * K, [P, 4, T])
        g_q = at("g_q", A + 8 * K, [P, 4, T])
        g_k = at("g_k", A + 12 * K, [P, 4, T])
        g_qe = at("g_qe", A + 16 * K, [P, 4, T])
        g_kd = at("g_kd", A + 20 * K, [P, 4, T])
        g_keep = at("g_keep", A + 24 * K, [P, 4, T])
        g_sc = at("g_sc", A + 28 * K, [P, TT, 4, P])
        v_tok = at("v_tok", B, [P, TT, 1024])
        k_tok = at("k_tok", B + 8 * K, [P, TT, 512])
        state = at("state", B + 12 * K, [P, 3, 1024])
        g_tmp = at("g_tmp", B + 24 * K, [P, TT, 4, P])
        g_el = at("g_el", B + 28 * K, [P, 4, 4])
        g_sq = at("g_sq", A, [P, 4, 2, T])
        g_rs = at("g_rs", A + 8 * K, [P, 4, T])
        g_y = at("g_y", A + 12 * K, [P, 8, T])
        n_sq = at("n_sq", A, [P, 12, T])
        n_rs = at("n_rs", A + 12 * K, [P, 4, T])
        n_x = at("n_x", HI, [P, 2, CMP_W, 2 * N_CMP])
        assert FIRST["out"] % 2 == 1
        prob = at("prob", A, [P, 8, 2, T])
        prob_t = at("prob_t", A + 16 * K, [P, 2, 5, P])
        v_nsa = at("v_nsa", B + 24 * K, [P, TT, 4, P])
        n_small = B + 8 * K
        hid = at("hid", n_small, [P, 2 * 2 * N_CMP])
        c_sq = at("c_sq", n_small + 256, [P, 2 * N_CMP])
        c_rs = at("c_rs", n_small + 384, [P, 2 * N_CMP])
        k_cmp = at("k_cmp", n_small + 512, [P, 2 * N_CMP])
        v_cmp = at("v_cmp", n_small + 640, [N_CMP, 2, P])
        gates = at("gates", n_small + 1664, [P, TT, 24])
        c_s = at("c_s", n_small + 1856, [P, TT, 8, N_CMP])
        c_mx = at("c_mx", n_small + 2816, [P, TT, 8])
        c_den = at("c_den", n_small + 2880, [P, TT, 8])
        c_p = at("c_p", n_small + 2944, [P, TT, 8, N_CMP])
        sg = at("sg", PR + 36 * K, [P, 2, T])
        gated = at("gated", PR + 38 * K, [P, 2, T])
        sq_tile = at("sq_tile", PR + 43 * K, [P, 2, T])
        e_sq = at("e_sq", B, [P, 12, T])
        e_rs = at("e_rs", B + 12 * K, [P, 4, T])
        e_rot = at("e_rot", B + 16 * K, [P, 2, 2, T])
        prob2 = at("prob2", B, [P, 8, 2, T])
        prob2_t = at("prob2_t", B + 16 * K, [P, 2, 5, P])
        v_ev = at("v_ev", B + 22 * K, [P, 2, TT, 4, P])
        f_a = at("f_a", PR + 16 * K, [P, 4, T + 8])
        f_b = at("f_b", PR + 21 * K, [P, 4, T + 8])
        pooled = at("pooled", PR + 26 * K, [P, 16, T])
        o_tok = at("o_tok", B, [P, TT, D])

        ps = stack.enter_context(nc.psum_tensor("ps", [P, 8, 512], F32))

        def con(name):
            a, w = CONS[name]
            return cons[:, a:a + w]

        def col(name, j=0, n=1):
            a, _ = COLS[name]
            return cols[:, a + j:a + j + n]

        def cbc(ap, n):
            return ap.rearrange("p (a w) -> p a w", a=1).to_broadcast([ap.shape[0], n, ap.shape[1]])

        def vbc(ap, n):
            return ap.rearrange("p (w a) -> p w a", a=1).to_broadcast([ap.shape[0], ap.shape[1], n])

        ident, ones = con("ident"), con("ones")

        raw_full = [S(f"raw_full{j}") for j in range(4)]
        side_full = [S(f"side_full{j}") for j in range(2)]
        hi_ready = S("hi_ready")
        lo_ready = S("lo_ready")
        halves_used = S("halves_used")
        mods_added = S("mods_added")
        mods_summed = S("mods_summed")
        cmp_used = S("cmp_used")
        dve_read = S("dve_read")
        silu_ready = S("silu_ready")

        ATT = {"n0": 0, "n1": 1, "a0": 2, "a1": 3, "b0": 4, "b1": 5}

        def att(name):
            kind, tt = name[0], int(name[1])
            a = {"kind": kind, "tt": tt, "base": 8 * ATT[name], "cols": slice(tt * P, tt * P + P)}
            if kind == "n":
                a["q"] = lambda h: NQ + h
                a["k"] = lambda h, part: (NKS, NKW)[part] + h // 4
                a["keys"] = (tt + 1) * P
                a["mask"] = [(part, tt, "above") for part in range(2)]
                a["v"] = lambda h, part, b: v_nsa[:, b, 2 * part + h // 4, :]
                a["prob"], a["prob_t"] = prob, prob_t
            else:
                off = 0 if kind == "a" else 4
                a["q"] = lambda h: 16 + 2 * off + h
                a["k"] = lambda h, part: 8 * part + off + h // 4
                a["keys"] = T
                a["mask"] = [] if kind == "a" else [(0, 1 - tt, "above" if tt == 0 else "below")]
                a["v"] = lambda h, part, b: v_ev[:, part, b, off // 2 + h // 4, :]
                a["prob"], a["prob_t"] = prob2, prob2_t
            a["blocks"] = [(part, b) for part in range(2) for b in range(a["keys"] // P)]
            return a

        block = stack.enter_context(nc.Block())

        @block.sync
        def _(sp):
            sp.dma_start(cons[:, 0:P], cons_in[:, 0:P]).then_inc(S("ident_in"), 16)
            for q in range(4):
                part = slice(q * D // 4, (q + 1) * D // 4)
                sp.dma_start(x_tok[:, :, part], x.rearrange("(a p) d -> p a d", p=P)[:, :, part])\
                  .then_inc(S(f"x_in{q}"), 16)
            sp.dma_start(cons[:, P:NCONS], cons_in[:, P:NCONS]).then_inc(S("const_in"), 16)
            sp.dma_start(cols[:, :], cols_in).then_inc(S("const_in"), 16)
            for h in range(4):
                sp.dma_start(raw[:, h, :], w_main[h]).then_inc(raw_full[h], 16)
            sp.dma_start(table[:, 0:7 * P], gla_masks_in).then_inc(S("small_in"), 16)
            sp.dma_start(gate_w2[0:16, :], gate_w2_in).then_inc(S("small_in"), 16)
            sp.dma_start(cmp_w2[:, :, :], cmp_w2_in).then_inc(S("small_in"), 16)

            def load(i, h):
                sp.wait_ge(lo_ready, i * 4 + (h - 3))
                src = w_main[h] if isinstance(i, int) else w_main[bass.ds(i * 4 + h, 1)].rearrange("a p n -> (a p) n")
                sp.dma_start(raw[:, h % 4, :], src).then_inc(raw_full[h % 4], 16)

            def side_load(i, n, free):
                if free is not None:
                    sp.wait_ge(*free)
                src = w_side[n] if isinstance(i, int) else w_side[bass.ds(i * 2 + n, 1)].rearrange("a p n -> (a p) n")
                sp.dma_start(side[:, n % 2, :], src).then_inc(side_full[n % 2], 16)

            def loads(stage, k0=0, k1=None, mods=False):
                k1 = COUNT[stage] if k1 is None else k1
                s0, s1 = FIRST[stage] + k0, min(FIRST[stage] + k1, STEPS - 2)

                def pair(i, k, count=2):
                    for c in range(count):
                        for half in range(2):
                            load(i, 2 * (s0 + k + c) + 4 + half)
                        if mods:
                            n, m = mod_half(stage, k0 + k + c)
                            side_load(i, n, None if m in (0, 1, CMP_AT, CMP_AT + 1) else (mods_added, i * 2 + (m - 1)))
                peel = 2 if mods and mod_half(stage, 0)[1] in (0, CMP_AT) else 0
                if peel:
                    if stage != MOD_STAGES[0]:
                        sp.wait_ge(cmp_used, 2 * CMP_HALVES)
                    pair(0, 0)
                with sp.Fori(0, (s1 - s0 - peel) // 2) as i:
                    pair(i, peel)
                if (s1 - s0) % 2:
                    pair(0, s1 - s0 - 1, 1)

            for stage, count in STAGES:
                if stage == "out":
                    for j in range(2 * CMP_HALVES):
                        side_load(0, CMP_AT + j, (mods_added, CMP_AT - 1 + j) if j < 2 else (cmp_used, j - 1))
                if stage == "down0":
                    sp.wait_ge(dve_read, dve_reads("down0"))
                    sp.dma_start(ctx_tok[:, :, :], ctx_in.rearrange("(a p) d -> p a d", p=P)).then_inc(S("ctx_in"), 16)
                    sp.dma_start(table[:, :], counts_in).then_inc(S("counts_in"), 16)
                if stage in MOD_GROUPS:
                    loads(stage, 0, DT, mods=True)
                    if count > DT:
                        loads(stage, DT)
                else:
                    loads(stage)
            for part in range(2):
                cut = slice(part * D // 2, (part + 1) * D // 2)
                for tt in range(TT):
                    sp.wait_ge(S(f"o_tok{tt}"), 2 * part + 2)
                    sp.dma_start(out[tt * P:(tt + 1) * P, cut], o_tok[:, tt, cut]).then_inc(S("stored"), 16)
            sp.wait_ge(S("stored"), 16 * 2 * TT)

        @block.tensor
        def _(pe):
            def half_products(out_ap, c, par, blocks, act_hi, act_lo, tile0, first, last, split=None):
                slot = 2 * par + c
                for n, b in enumerate(blocks):
                    wh, wl = w_hi[:, slot, b * P:(b + 1) * P], w_lo[:, slot, b * P:(b + 1) * P]
                    kt = tile0 + n
                    if split is not None:
                        pe.wait_ge(S(split[0]), split[1] + kt + 1)
                    pe.matmul(out_ap, wh, act_hi[:, kt, :], start=first and n == 0, stop=False)
                    pe.matmul(out_ap, wh, act_lo[:, kt, :], start=False, stop=False)
                    mm = pe.matmul(out_ap, wl, act_hi[:, kt, :], start=False, stop=last and n == len(blocks) - 1)
                return mm

            def step(stage, i, k, act, kt=16, free=None, second=None, split=None):
                s = FIRST[stage] + k
                par = s % 2
                if free is not None:
                    pe.wait_ge(*free)
                for c in range(2):
                    pe.wait_ge(lo_ready, i * 4 + (2 * s + c + 1))
                    nb = min(8, kt - 8 * c)
                    splits = split or [None, None]
                    mm = half_products(ps[:, par, 0:T], c, par, range(nb), *act, 8 * c, c == 0, c == 1, splits[0])
                    if second is not None:
                        mm = half_products(ps[:, 2 + par, 0:T], c, par, range(nb), *second, 8 * c, c == 0, c == 1,
                                           splits[1])
                    mm.then_inc(halves_used, 1)

            def run(stage, act, kt=16, second=None, split=None, summed=None):
                base = dve_reads(stage)

                def sum_squares(k):
                    return pe.matmul(ps[:, 2, 0:T], ones, sq_tile[:, k % 2, :], start=k == 0, stop=k == COUNT[stage] - 1)

                def body(i, k):
                    step(stage, i, k, act, kt, None if base + k < 2 else (dve_read, i * 2 + (base + k - 1)), second,
                         split if isinstance(i, int) and k == 0 else None)
                    if summed is not None and k:
                        pe.wait_ge(S(f"{summed}_sq"), i * 2 + k)
                        sum_squares(k - 1)
                steps(pe, stage, body, first=2 if split or summed else 0)
                if summed is not None:
                    pe.wait_ge(S(f"{summed}_sq"), COUNT[stage])
                    sum_squares(COUNT[stage] - 1).then_inc(S(f"{summed}_ms"), 1)
                if stage in MOD_GROUPS:
                    sum_mods(stage)

            def run_z(stage, done):
                def body(i, k):
                    step(stage, i, k, (a_hi, a_lo), free=(silu_ready, i * 2 + (FFN_TILES + done + k)))
                steps(pe, stage, body)
                if stage in MOD_GROUPS:
                    sum_mods(stage)

            def sum_mods(stage):
                g = MOD_STAGES.index(stage)
                pe.wait_ge(mods_added, DT * (g + 1))
                vecs = 2 if MOD_GROUPS[stage] in BOTH else 1
                for t in range(8):
                    for c in range(vecs):
                        mm = pe.matmul(ps[:, 7, vecs * t + c:vecs * t + c + 1], mod_sum[:, c, t * P:(t + 1) * P],
                                       ones[:, 0:1], start=True, stop=True)
                mm.then_inc(mods_summed, 1)

            def turn(src_ap, bank, at_col, rows=P, ncols=P, base=0):
                return pe.transpose(ps[0:ncols, bank, at_col:at_col + rows], src_ap, ident[base:base + rows, base:base + rows])

            def norm(name, bank=2):
                for q in range(4):
                    pe.wait_ge(S(f"{name}_sq"), q + 1)
                    for f in range(4 * q, 4 * q + 4):
                        src = sq2 if name == "ctx" else sq
                        mm = pe.matmul(ps[:, bank, 0:T], ones, src[:, f, :], start=f == 0, stop=f == 15)
                mm.then_inc(S(f"{name}_ms"), 1)

            def token_to_feature(name):
                tok = x_tok if name == "x" else ctx_tok
                for g in range(8):
                    if name == "x" and g % 2 == 0:
                        pe.wait_ge(S(f"x_in{g // 2}"), 16)
                    for f in range(2 * g, 2 * g + 2):
                        for tt in range(TT):
                            mm = turn(tok[:, tt, f * P:(f + 1) * P], g, (f % 2) * T + tt * P)
                    mm.then_inc(S(f"{name}_t"), 1)

            pe.wait_ge(S("ident_in"), 16)
            token_to_feature("x")
            pe.wait_ge(S("const_in"), 32)
            norm("attn")
            run("conv", (a_hi, a_lo), split=[("attn_lo", 0)])
            run("rest", (a_hi, a_lo))

            pe.wait_ge(S("small_in"), 48)
            pe.wait_ge(dve_read, dve_reads("out"))
            for h in range(4):
                mm = pe.matmul(ps[:, 2 + h // 2, (h % 2) * T:(h % 2 + 1) * T], gate_w2[0:16, h * P:(h + 1) * P],
                               pr[0:16, LAST, :], start=True, stop=True)
            mm.then_inc(S("g_z"), 1)

            def gla_scores(q, k):
                for tt in range(TT):
                    for h in range(4):
                        mm = pe.matmul(ps[:, 4 + tt, h * P:(h + 1) * P], k(h)[:, tt * P:(tt + 1) * P],
                                       q(h)[:, tt * P:(tt + 1) * P], start=True, stop=True)
                return mm

            pe.wait_ge(S("g_silu"), 2)
            gla_scores(lambda h: pr[:, QT + h, :], lambda h: pr[:, KT + h, :]).then_inc(S("g_s"), 1)
            def compress(c):
                pe.wait_ge(side_full[(CMP_AT + c) % 2], 16 * ((CMP_AT + c) // 2 + 1))
                kv = c // CMP_HALVES
                for b in range(8):
                    j = 8 * (c % CMP_HALVES) + b
                    mm = pe.matmul(ps[:, 7, 32 * kv:32 * kv + 2 * N_CMP], side[:, (CMP_AT + c) % 2, b * P:(b + 1) * P],
                                   n_x[:, kv, j, :], start=j == 0, stop=j == CMP_W - 1)
                mm.then_inc(cmp_used, 1)

            pe.wait_ge(S("g_v"), 3)
            for tt in range(TT):
                for f in range(8):
                    mm = turn(pr[:, VT + f, tt * P:(tt + 1) * P], 2 * tt + f // 4, (f % 4) * P)
            mm.then_inc(S("g_vt"), 1)
            pe.wait_ge(S("n_xr"), 2)
            compress(0)
            for lv in range(LEVELS):
                pe.wait_ge(S("g_mul"), 2 * (lv + 1))
                pe.wait_ge(S("g_msk"), 2 * (lv + 1))
                gla_scores(lambda h: g_q[:, h, :], lambda h: g_k[:, h, :]).then_inc(S("g_s"), 1)
                compress(lv + 1)
            pe.wait_ge(S("g_vtok"), 2)
            pe.wait_ge(S("g_kdr"), 1)
            for tt in range(TT):
                for h in range(4):
                    mm = turn(g_kd[:, h, tt * P:(tt + 1) * P], 2 + tt, h * P)
            mm.then_inc(S("g_kt"), 1)
            compress(LEVELS + 1)
            pe.wait_ge(S("g_ktok"), 1)
            for c in range(3):
                tt, r0 = c // 2, (c % 2) * CHUNK
                for h in range(4):
                    mm = pe.matmul(ps[:, 2 * (c % 2) + h // 2, (h % 2) * 256:(h % 2 + 1) * 256],
                                   k_tok[r0:r0 + CHUNK, tt, h * P:(h + 1) * P],
                                   v_tok[r0:r0 + CHUNK, tt, h * 256:(h + 1) * 256], start=True, stop=True)
                mm.then_inc(S("g_kv"), 1)
                if c == 1:
                    pe.wait_ge(S("g_state"), 1)
            pe.wait_ge(S("g_state"), 3)
            pe.wait_ge(S("g_add"), 2 * LEVELS)
            for h in range(4):
                bank, started = O_BANKS[h], False
                for e in range(2):
                    rows = slice(h * 256 + e * P, h * 256 + (e + 1) * P)
                    for tt in range(TT):
                        o_ap = ps[:, bank, e * T + tt * P:e * T + (tt + 1) * P]
                        pe.matmul(o_ap, v_tok[:, tt, rows], g_sc[:, tt, h, :], start=not started, stop=False,
                                  skip_group_check=True)
                        started = True
                        for c in (2 * tt, 2 * tt + 1):
                            if c == 0:
                                continue
                            mm = pe.matmul(ps[:, bank, e * T + c * CHUNK:e * T + (c + 1) * CHUNK],
                                           state[:, c - 1, rows], g_qe[:, h, c * CHUNK:(c + 1) * CHUNK],
                                           start=False, stop=e == 1 and c == 3, skip_group_check=True)
                mm.then_inc(S("g_o"), 1)
            pe.wait_ge(S("g_sqr"), 4)
            for p2 in range(2):
                for e in range(2):
                    mm = pe.matmul(ps[:, 4 + p2, 0:2 * T], ones, g_sq[:, 2 * p2:2 * p2 + 2, e, :],
                                   start=e == 0, stop=e == 1)
            mm.then_inc(S("g_ms"), 1)

            def query_sums(sq_t, bank):
                for tt in range(TT):
                    for h in range(8):
                        mm = pe.matmul(ps[:, bank, 8 * tt + h:8 * tt + h + 1], sq_t[:, 4 + h, tt * P:(tt + 1) * P],
                                       ones[:, 0:1], start=True, stop=True)
                return mm

            pe.wait_ge(S("g_out"), 1)
            pe.wait_ge(S("n_sqr"), 1)
            for p2 in range(2):
                mm = pe.matmul(ps[:, p2, :], ones, n_sq[:, 2 * p2:2 * p2 + 2, :], start=True, stop=True)
            query_sums(n_sq, 5).then_inc(S("n_ms"), 1)
            for tt in range(TT):
                mm = turn(pr[GATE_ROW:GATE_ROW + 24, LAST, tt * P:(tt + 1) * P], 6, 32 * tt, rows=24, base=GATE_ROW)
            mm.then_inc(S("n_gt"), 1)
            pe.wait_ge(S("n_hs"), 1)
            pe.wait_ge(S("n_gs"), 1)
            mm = pe.matmul(ps[:, 6, 0:2 * N_CMP], cmp_w2[:, 0, :], hid[:, 0:2 * N_CMP], start=True, stop=True)
            mm.then_inc(S("n_kc"), 1)
            for kv in range(2):
                mm = pe.matmul(ps[0:N_CMP, 4, kv * P:(kv + 1) * P],
                               hid[:, (2 + kv) * N_CMP:(3 + kv) * N_CMP], cmp_w2[:, 1, :], start=True, stop=True)
            mm.then_inc(S("n_vc"), 1)
            pe.wait_ge(S("n_csq"), 1)
            pe.wait_ge(S("n_msr"), 1)
            mm = pe.matmul(ps[:, 2, 0:2 * N_CMP], ones, c_sq[:, :], start=True, stop=True)
            mm.then_inc(S("n_cms"), 1)
            for tt in range(TT):
                for f in range(4):
                    mm = turn(pr[:, NVS + f, tt * P:(tt + 1) * P], tt, f * P)
            mm.then_inc(S("n_vt"), 1)
            pe.wait_ge(S("n_qk"), 2)
            pe.wait_ge(S("n_kcn"), 1)
            for tt in range(TT):
                for h in range(8):
                    mm = pe.matmul(ps[:, 2 + tt, 16 * h:16 * h + N_CMP], pr[:, NQ + h, tt * P:(tt + 1) * P],
                                   k_cmp[:, (h // 4) * N_CMP:(h // 4 + 1) * N_CMP], start=True, stop=True)
            mm.then_inc(S("n_cs"), 1)

            def attend(name):
                a = att(name)
                base = a["base"]
                if base:
                    pe.wait_ge(S("at_out"), base)
                for h in range(8):
                    if h >= 3:
                        pe.wait_ge(S("at_exp"), base + h - 2)
                    for part in range(2):
                        mm = pe.matmul(ps[:, 2 + h % 3, part * T:part * T + a["keys"]],
                                       pr[:, a["q"](h), a["cols"]], pr[:, a["k"](h, part), 0:a["keys"]],
                                       start=True, stop=True)
                    mm.then_inc(S("at_sc"), 1)

                def values(h):
                    pe.wait_ge(S("at_pt"), base + h + 1)
                    if h >= 2:
                        pe.wait_ge(S("at_out"), base + h - 1)
                    blocks = a["blocks"]
                    for n, (part, b) in enumerate(blocks):
                        mm = pe.matmul(ps[:, 5 + h % 2, 0:P], a["v"](h, part, b), a["prob_t"][:, h % 2, n, :],
                                       start=n == 0, stop=a["kind"] != "n" and n == len(blocks) - 1)
                    if a["kind"] == "n":
                        mm = pe.matmul(ps[:, 5 + h % 2, 0:P], v_cmp[:, h // 4, :], a["prob_t"][0:N_CMP, h % 2, 4, :],
                                       start=False, stop=True)
                    mm.then_inc(S("at_pv"), 1)

                pe.wait_ge(S("at_exp"), base + 8)
                for h in range(8):
                    pe.wait_ge(S("at_scl"), base + h + 1)
                    if h >= 2:
                        pe.wait_ge(S("at_pt"), base + h - 1)
                    for n, (part, b) in enumerate(a["blocks"]):
                        mm = turn(a["prob"][:, h, part, b * P:(b + 1) * P], h % 2, n * P)
                    if a["kind"] == "n":
                        mm = turn(c_p[:, a["tt"], h, :], 2 + h % 2, 0, ncols=N_CMP)
                    mm.then_inc(S("at_t"), 1)
                    if h:
                        values(h - 1)
                values(7)

            pe.wait_ge(S("n_vtok"), 1)
            pe.wait_ge(S("c_ready"), 2)
            attend("n0")
            attend("n1")

            pe.wait_ge(S("mix_lo"), 1)
            run("out", (b_hi, b_lo), summed="ffn")

            for c, n in enumerate(CHUNKS):
                silus = sum(CHUNKS[:c])
                pe.wait_ge(dve_read, dve_reads(f"up{c}"))

                def body(i, k, c=c, silus=silus):
                    step(f"up{c}", i, k, (a_hi, a_lo),
                         free=(S("gate_y"), i + (silus + 1)) if k % 2 else (silu_ready, i + (silus + 1)),
                         split=[("ffn_lo", 0)] if c == 0 and isinstance(i, int) and k == 0 else None)
                steps(pe, f"up{c}", body, first=0 if c else 2)
                sum_mods(f"up{c}")
                run(f"down{c}", (b_hi, b_lo), kt=n, split=[("gate_lo", silus)],
                    summed="ev" if c == len(CHUNKS) - 1 else None)

            pe.wait_ge(S("ctx_in"), 16)
            pe.wait_ge(S("ev_rs"), 3)
            token_to_feature("ctx")
            norm("ctx")
            run("ev_kv", (a_hi, a_lo), second=(b_hi, b_lo), split=[("ev_lo", 0), ("ctx_lo", 0)])
            run("ev_q", (a_hi, a_lo))
            pe.wait_ge(S("e_sqr"), 3)
            for p2 in range(2):
                mm = pe.matmul(ps[:, 2 + p2, :], ones, e_sq[:, 2 * p2:2 * p2 + 2, :], start=True, stop=True)
            query_sums(e_sq, 6).then_inc(S("e_ms"), 1)
            for src in range(2):
                for tt in range(TT):
                    for f in range(4):
                        tile = 8 * src + (2, 3, 6, 7)[f]
                        mm = turn(pr[:, tile, tt * P:(tt + 1) * P], V_BANKS[2 * src + tt], f * P)
            mm.then_inc(S("e_vt"), 1)
            pe.wait_ge(S("e_nrm"), 2)
            for n, t0 in enumerate(ROPE_PAIRS):
                if n >= 3:
                    pe.wait_ge(S("e_rot"), n - 2)
                w = rot_g[:, 0, :] if 16 <= t0 < 24 else con("rot")
                pe.matmul(ps[:, ROPE_BANKS[n % 3], :], w, pr[:, t0:t0 + 2, :], start=True, stop=True)\
                  .then_inc(S("e_rp"), 1)
            pe.wait_ge(S("e_rope"), len(ROPE_PAIRS))
            pe.wait_ge(S("e_vtok"), 4)
            for name in ("a0", "a1", "b0", "b1"):
                attend(name)
            pe.wait_ge(S("at_out"), 48)
            run_z("ev_z", 0)
            run("ev_out", (b_hi, b_lo), split=[("gate_lo", FFN_TILES)], summed="ev_post")

            norm("od")
            run("od_u", (a_hi, a_lo), split=[("od_lo", 0)])
            base = dve_reads("pool")
            pe.wait_ge(dve_read, base)
            for g in range(4):
                s = FIRST["pool"] + g
                par = s % 2
                pe.wait_ge(S("pool_lo"), g + 1)
                if g >= 2:
                    pe.wait_ge(dve_read, base + g - 1)
                for c in range(2):
                    pe.wait_ge(lo_ready, 2 * s + c + 1)
                    for n in range(2):
                        mm = half_products(ps[:, 2 * par + c, n * T:(n + 1) * T], c, par, range(4 * n, 4 * n + 4),
                                           b_hi, b_lo, 4 * g, True, True)
                    mm.then_inc(halves_used, 1)
            pe.wait_ge(dve_read, base + 4)
            run_z("od_z", 16)
            run("od_out", (b_hi, b_lo), split=[("gate_lo", FFN_TILES + 16)], summed="od_post")
            for g in range(4):
                pe.wait_ge(S("final"), g + 1)
                for tt in range(TT):
                    for f in range(4 * g, 4 * g + 4):
                        mm = turn(res[:, f, tt * P:(tt + 1) * P], 4 * tt + g, (f % 4) * P)
                    mm.then_inc(S("o_t"), 1)

        def gate_silu_steps(act, stage, silus):
            def extra(i, k):
                if k % 2:
                    return
                s = FIRST[stage] + k
                act.wait_ge(halves_used, i * 4 + (2 * s + 2))
                act.wait_ge(S("gate_y"), i + (silus + 1))
                act.activation(sg[:, 0, :], ps[:, s % 2, 0:T], ACT.Silu).then_inc(silu_ready, 1)
            return extra

        def z_silu_steps(act, stage, done):
            def extra(i, k):
                s = FIRST[stage] + k
                act.wait_ge(halves_used, i * 4 + (2 * s + 2))
                act.wait_ge(S("gate_y"), i * 2 + (FFN_TILES + done + k + 1))
                act.activation(sg[:, 0, :], ps[:, s % 2, 0:T], ACT.Silu).then_inc(silu_ready, 1)
            return extra

        @block.scalar
        def _(act):
            def hi(i, s):
                for c in range(2):
                    slot = 2 * (s % 2) + c
                    act.wait_ge(raw_full[slot], i * 16 + 16 * (s // 2 + 1))
                    if s >= 2:
                        act.wait_ge(halves_used, i * 4 + (2 * s + c - 3))
                    act.activation(w_hi[:, slot, :], raw[:, slot, :], ACT.Copy).then_inc(hi_ready, 1)

            def ahead(stage, first=0, extra=None, squared=None, of=None):
                base = dve_reads(stage)

                def square(i, k):
                    act.wait_ge(dve_read, i * 2 + (base + k + 1))
                    src = of[:, k:k + 1, :] if isinstance(i, int) else of[:, bass.ds(i * 2 + k, 1), :]
                    act.activation(sq_tile[:, k % 2:k % 2 + 1, :], src, ACT.Square).then_inc(S(f"{squared}_sq"), 1)

                def body(i, k):
                    if FIRST[stage] + k + 1 < STEPS:
                        hi(i, FIRST[stage] + k + 1)
                    if extra is not None:
                        extra(i, k)
                    if squared is not None and k:
                        square(i, k - 1)
                if squared is not None:
                    first = 2
                steps(act, stage, body, first=first, last=2 if stage == "od_out" else 0)
                if squared is not None:
                    square(0, COUNT[stage] - 1)

            def squares(name, src, dst, wait):
                for q in range(4):
                    wait(q)
                    act.activation(dst[:, 4 * q:4 * q + 4, :], src[:, 4 * q:4 * q + 4, :], ACT.Square)\
                       .then_inc(S(f"{name}_sq"), 1)

            def root(name, buf):
                act.wait_ge(S(f"{name}_rs"), 1)
                act.activation(buf, buf, ACT.Sqrt).then_inc(S(f"{name}_rs"), 1)

            def shift_hi(name, y, dst, shift):
                for f in range(16):
                    act.wait_ge(S(f"{name}_y"), f + 1)
                    if shift is None:
                        ins = act.activation(dst[:, f, :], y[:, f, :], ACT.Copy)
                    else:
                        ins = act.activation(dst[:, f, :], y[:, f, :], ACT.Identity, bias=shift(f))
                    ins.then_inc(S(f"{name}_hi"), 1)

            def from_psum(name, dst):
                for g in range(0, 8, 2):
                    act.wait_ge(S(f"{name}_t"), g + 1)
                    act.activation(dst[:, 2 * g:2 * g + 2, :], ps[:, g, :], ACT.Copy).then_inc(S(f"{name}_fa"), 1)

            act.wait_ge(S("const_in"), 32)
            from_psum("x", res)
            squares("attn", res, sq, lambda q: (act.wait_ge(S("x_fa"), q + 1), act.wait_ge(S("x_fd"), q + 1)))
            hi(0, 0)
            act.activation(csil[:, :, :], col("cvec", 0, 32).rearrange("p (t c) -> p t c", c=2), ACT.Silu)\
               .then_inc(S("csil"), 1)
            root("attn", rstd[:, :])
            shift_hi("attn", sq, a_hi, None)
            ahead("conv", first=2)

            def conv_silu(i, k):
                if k % 2 == 0 and k < 28:
                    act.activation(pr[:, bass.ds(i, 1), :], pr[:, bass.ds(i, 1), :], ACT.Silu)
            act.wait_ge(dve_read, 16)
            ahead("rest", extra=conv_silu)
            act.activation(pr[:, 14:16, :], pr[:, 14:16, :], ACT.Silu).then_inc(S("g_silu"), 1)
            act.wait_ge(dve_read, dve_reads("out"))
            act.activation(pr[:, GOUT:GOUT + 8, :], pr[:, GOUT:GOUT + 8, :], ACT.Silu).then_inc(S("g_silu"), 1)

            act.wait_ge(S("g_z"), 1)
            for h in range(4):
                ins = act.activation(g_d[:, h, :], ps[:, 2 + h // 2, (h % 2) * T:(h % 2 + 1) * T], ACT.Abs,
                                     bias=col("gate_b", h))
            ins.then_inc(S("g_soft"), 1)
            act.wait_ge(S("g_soft"), 1)
            act.activation(g_d[:, :, :], g_d[:, :, :], ACT.Exp, scale=-1.0).then_inc(S("g_soft"), 1)
            act.wait_ge(S("g_soft"), 2)
            act.activation(g_d[:, :, :], g_d[:, :, :], ACT.Ln, bias=1.0).then_inc(S("g_soft"), 1)
            act.wait_ge(S("g_vt"), 1)
            for tt in range(TT):
                act.activation(v_tok[:, tt, :], ps[:, 2 * tt:2 * tt + 2, :].rearrange("p a n -> p (a n)"), ACT.Copy)\
                   .then_inc(S("g_vtok"), 1)
            for n in range(LEVELS + 1):
                act.wait_ge(S("g_diff"), 2 * (n + 1) if n < LEVELS else 2 * LEVELS + 1)
                act.activation(g_d[:, :, :], g_d[:, :, :], ACT.Exp, scale=1.0 / TAU).then_inc(S("g_dec"), 1)
            act.wait_ge(S("g_kdr"), 1)
            act.activation(g_d[:, :, :], g_b[:, :, :], ACT.Exp, scale=1.0 / TAU).then_inc(S("g_dec"), 1)
            act.activation(g_el[:, :, :], g_b[:, :, CHUNK - 1:T:CHUNK], ACT.Exp, scale=1.0 / TAU)\
               .then_inc(S("g_dec"), 1)
            act.wait_ge(S("g_kt"), 1)
            act.activation(k_tok[:, :, :], ps[:, 2:4, :], ACT.Copy).then_inc(S("g_ktok"), 1)
            for h in range(4):
                act.wait_ge(S("g_o"), h + 1)
                act.activation(g_sq[:, h, :, :], ps[:, O_BANKS[h], :].rearrange("p (e t) -> p e t", e=2),
                               ACT.Square).then_inc(S("g_sqr"), 1)
            act.wait_ge(S("g_rsr"), 1)
            act.activation(g_rs[:, :, :], g_rs[:, :, :], ACT.Sqrt).then_inc(S("g_rsr"), 1)
            act.wait_ge(S("g_yr"), 9)
            act.activation(b_hi[:, 0:8, :], g_y[:, :, :], ACT.Copy).then_inc(S("g_hi"), 1)

            act.wait_ge(S("g_out"), 1)
            act.activation(n_sq[:, 0:4, :], pr[:, NKS:NKS + 4, :], ACT.Square)
            act.activation(n_sq[:, 4:12, :], pr[:, NQ:NQ + 8, :], ACT.Square).then_inc(S("n_sqr"), 1)
            act.wait_ge(S("n_gt"), 1)
            act.activation(gates[:, :, :], ps[:, 6, 0:64].rearrange("p (a b) -> p a b", a=2)[:, :, 0:24],
                           ACT.Sigmoid).then_inc(S("n_gs"), 1)
            act.wait_ge(cmp_used, 2 * CMP_HALVES)
            act.activation(hid[:, :].rearrange("p (a b) -> p a b", a=2),
                           ps[:, 7, 0:64].rearrange("p (a b) -> p a b", a=2)[:, :, 0:2 * N_CMP], ACT.Silu)\
               .then_inc(S("n_hs"), 1)
            act.wait_ge(S("n_kc"), 1)
            act.activation(c_sq[:, :], ps[:, 6, 0:2 * N_CMP], ACT.Square).then_inc(S("n_csq"), 1)
            act.wait_ge(S("n_msr"), 1)
            act.activation(q_rs[:, :, :], q_rs[:, :, :], ACT.Sqrt)
            act.activation(n_rs[:, :, :], n_rs[:, :, :], ACT.Sqrt).then_inc(S("n_rt"), 1)
            act.wait_ge(S("n_crs"), 1)
            act.activation(c_rs[:, :], c_rs[:, :], ACT.Sqrt).then_inc(S("n_crt"), 1)
            act.wait_ge(S("n_vt"), 1)
            act.activation(v_nsa[:, :, :, :], ps[:, 0:2, :].rearrange("p a (f n) -> p a f n", f=4), ACT.Copy)\
               .then_inc(S("n_vtok"), 1)
            for tt in range(TT):
                act.wait_ge(S("c_sub"), tt + 1)
                act.activation(c_s[:, tt, :, :], c_s[:, tt, :, :], ACT.Exp).then_inc(S("c_exp"), 1)

            def attend(name):
                a = att(name)
                base = a["base"]
                for h in range(8):
                    act.wait_ge(S("at_nb_r"), base + h + 1)
                    src = ps[:, 2 + h % 3, :].rearrange("p (a n) -> p a n", a=2)
                    scale = SCALE if a["kind"] == "b" else q_rs[:, a["tt"], h:h + 1]
                    if a["kind"] == "n":
                        for part in range(2):
                            ins = act.activation(a["prob"][:, h, part, 0:a["keys"]], src[:, part, 0:a["keys"]],
                                                 ACT.Exp, bias=at_nb[:, 2 * h + part:2 * h + part + 1], scale=scale,
                                                 accum_out=at_den[:, 2 * h + part:2 * h + part + 1])
                    else:
                        ins = act.activation(a["prob"][:, h, :, :], src, ACT.Exp, bias=at_nb[:, h:h + 1],
                                             scale=scale, accum_out=at_den[:, h:h + 1])
                    ins.then_inc(S("at_exp"), 1)
                if a["kind"] == "b":
                    act.wait_ge(S("at_sd"), a["tt"] + 1)
                    act.activation(at_sink[:, :], at_sink[:, :], ACT.Exp).then_inc(S("at_se"), 1)
                for h in range(8):
                    act.wait_ge(S("at_t"), base + h + 1)
                    if h >= 2:
                        act.wait_ge(S("at_pv"), base + h - 1)
                    n = len(a["blocks"])
                    if a["kind"] == "n":
                        act.activation(a["prob_t"][0:N_CMP, h % 2, 4, :], ps[0:N_CMP, 2 + h % 2, 0:P], ACT.Copy)
                    act.activation(a["prob_t"][:, h % 2, 0:n, :],
                                   ps[:, h % 2, 0:n * P].rearrange("p (a n) -> p a n", n=P), ACT.Copy)\
                       .then_inc(S("at_pt"), 1)

            attend("n0")
            attend("n1")
            act.wait_ge(S("at_out"), 16)
            act.activation(b_hi[:, 8:16, :], pr[:, NQ:NQ + 8, :], ACT.Copy).then_inc(S("mix_hi"), 1)

            ahead("out", squared="ffn", of=res)
            root("ffn", rstd[:, :])
            shift_hi("ffn", sq, a_hi, None)
            act.activation(sg[:, 1, 0:2], ident[:, 0:2], ACT.Copy).then_inc(silu_ready, 1)
            for c, n in enumerate(CHUNKS):
                ahead(f"up{c}", extra=gate_silu_steps(act, f"up{c}", sum(CHUNKS[:c])))
                if c < len(CHUNKS) - 1:
                    ahead(f"down{c}")
                else:
                    ahead(f"down{c}", squared="ev", of=res)

            root("ev", rstd[:, :])
            shift_hi("ev", sq, a_hi, lambda f: mods[:, f, 0:1])
            act.wait_ge(S("ev_lo"), 16)
            from_psum("ctx", ctx_f)
            act.wait_ge(S("ctx_t"), 8)
            squares("ctx", ctx_f, sq2, lambda q: (act.wait_ge(S("ctx_fa"), q + 1), act.wait_ge(S("ctx_fd"), q + 1)))
            root("ctx", rstd[:, :])
            shift_hi("ctx", sq2, b_hi, lambda f: mods[:, f, 1:2])
            ahead("ev_kv")
            ahead("ev_q")
            act.wait_ge(dve_read, dve_reads("ev_z"))
            for dst, src in ((slice(0, 2), slice(0, 2)), (slice(2, 4), slice(8, 10)), (slice(4, 12), slice(16, 24))):
                act.activation(e_sq[:, dst, :], pr[:, src, :], ACT.Square).then_inc(S("e_sqr"), 1)
            act.wait_ge(S("e_msr"), 1)
            act.activation(q_rs[:, :, :], q_rs[:, :, :], ACT.Sqrt)
            act.activation(e_rs[:, :, :], e_rs[:, :, :], ACT.Sqrt).then_inc(S("e_rt"), 1)
            act.wait_ge(S("e_vt"), 1)
            for n in range(4):
                act.activation(v_ev[:, n // 2, n % 2, :, :], ps[:, V_BANKS[n], :].rearrange("p (f n) -> p f n", f=4),
                               ACT.Copy).then_inc(S("e_vtok"), 1)
            for name in ("a0", "a1", "b0", "b1"):
                attend(name)
            ahead("ev_z", extra=z_silu_steps(act, "ev_z", 0))
            ahead("ev_out", squared="ev_post", of=pr)
            root("ev_post", rstd[:, :])

            squares("od", res, sq, lambda q: act.wait_ge(S("ev_res"), q + 1))
            root("od", rstd[:, :])
            shift_hi("od", sq, a_hi, lambda f: mods[:, 48 + f, 0:1])
            ahead("od_u")
            for g in range(4):
                act.wait_ge(S("pool_y"), g + 1)
                act.activation(b_hi[:, 4 * g:4 * g + 4, :], pooled[:, 4 * g:4 * g + 4, :], ACT.Copy)\
                   .then_inc(S("pool_hi"), 1)
            for k in range(4):
                hi(0, FIRST["pool"] + k + 1)
            ahead("od_z", extra=z_silu_steps(act, "od_z", 16))
            ahead("od_out", squared="od_post", of=pr)
            root("od_post", rstd[:, :])
            for g in range(4):
                act.wait_ge(S("o_t"), 2 * g + 1)
                act.activation(o_tok[:, 0, g * 512:(g + 1) * 512], ps[:, g, :], ACT.Copy).then_inc(S("o_tok0"), 1)

        @block.vector
        def _(dve):
            def lo(i, s):
                for c in range(2):
                    slot = 2 * (s % 2) + c
                    dve.wait_ge(hi_ready, i * 4 + (2 * s + c + 1))
                    dve.tensor_tensor(w_lo[:, slot, :], raw[:, slot, :], w_hi[:, slot, :].bitcast(F32), ALU.subtract)\
                       .then_inc(lo_ready, 1)

            def add_mod(stage, i, k):
                n, m = mod_half(stage, k)
                vecs = 2 if MOD_GROUPS[stage] in BOTH else 1
                dve.wait_ge(side_full[n % 2], i * 16 + 16 * (n // 2 + 1))
                if k or not isinstance(i, int):
                    dve.wait_ge(mods_added, i * 2 + m)
                for c in range(vecs):
                    value = csil[:, k:k + 1, c] if isinstance(i, int) else csil[:, bass.ds(i * 2 + k, 1), c]
                    ins = dve.scalar_tensor_tensor(out=mod_sum[:, c, :], in0=side[:, n % 2, :], scalar=value,
                                                   in1=mod_sum[:, c, :], op0=ALU.mult, op1=ALU.add)
                ins.then_inc(mods_added, 1)

            def clear_mods(g):
                dve.memset(mod_sum[:, :, :], 0.0).then_inc(S("mods_clear"), 1)
                dve.wait_ge(S("mods_clear"), g + 1)

            def reading(stage, read, first=0, splits=(), between=None):
                def body(i, k):
                    s = FIRST[stage] + k
                    if s + 1 < STEPS:
                        lo(i, s + 1)
                    if stage in MOD_GROUPS and k < DT:
                        add_mod(stage, i, k)
                    dve.wait_ge(halves_used, i * 4 + (2 * s + 2))
                    read(i, k, s % 2)
                steps(dve, stage, body, first=first, last=2 if stage == "od_out" else 0,
                      splits=[DT] if stage in MOD_GROUPS else splits, between=between)
                if stage in MOD_GROUPS:
                    g, t0 = MOD_STAGES.index(stage), 8 * MOD_GROUPS[stage]
                    vecs = 2 if MOD_GROUPS[stage] in BOTH else 1
                    dve.wait_ge(mods_summed, g + 1)
                    dve.tensor_tensor(mods[:, t0:t0 + 8, 0:vecs],
                                      ps[:, 7, 0:8 * vecs].rearrange("p (m c) -> p m c", c=vecs),
                                      vbc(col("mod_b", t0, 8), vecs), ALU.add).then_inc(S("mods_read"), 1)
                    if g + 1 < len(MOD_STAGES):
                        clear_mods(g + 1)

            def tile(t, i, k):
                return t[:, k:k + 1, :] if isinstance(i, int) else t[:, bass.ds(i * 2 + k, 1), :]

            def psum_tile(bank):
                return ps[:, bank:bank + 1, 0:T]

            def mean_to_rstd(name, src, dst, width):
                dve.wait_ge(S(f"{name}_ms"), 1)
                dve.tensor_scalar(dst, src, 1.0 / width, EPS, ALU.mult, ALU.add).then_inc(S(f"{name}_rs"), 1)
                dve.wait_ge(S(f"{name}_rs"), 2)
                dve.reciprocal(dst, dst).then_inc(S(f"{name}_rs"), 1)
                dve.wait_ge(S(f"{name}_rs"), 3)

            def norm(name, src, y, gain, shift, hi_t, lo_t):
                mean_to_rstd(name, ps[:, 2, 0:T], rstd[:, :], D)
                for n in range(18):
                    if n < 16:
                        dve.scalar_tensor_tensor(out=y[:, n, :], in0=src[:, n, :], scalar=gain(n), in1=rstd[:, :],
                                                 op0=ALU.mult, op1=ALU.mult).then_inc(S(f"{name}_y"), 1)
                    f = n - 2
                    if f < 0:
                        continue
                    dve.wait_ge(S(f"{name}_hi"), f + 1)
                    h = hi_t[:, f, :].bitcast(F32)
                    if shift is None:
                        ins = dve.tensor_tensor(lo_t[:, f, :], y[:, f, :], h, ALU.subtract)
                    else:
                        ins = dve.scalar_tensor_tensor(out=lo_t[:, f, :], in0=y[:, f, :], scalar=shift(f), in1=h,
                                                       op0=ALU.add, op1=ALU.subtract)
                    ins.then_inc(S(f"{name}_lo"), 1)

            def post_norm(name, gate, done):
                mean_to_rstd(name, ps[:, 2, 0:T], rstd[:, :], D)
                for q in range(5):
                    if q < 4:
                        for f in range(4 * q, 4 * q + 4):
                            ins = dve.scalar_tensor_tensor(out=sq2[:, f, :], in0=pr[:, f, :], scalar=gate[:, f:f + 1],
                                                           in1=rstd[:, :], op0=ALU.mult, op1=ALU.mult)
                        ins.then_inc(S(f"{name}_y"), 1)
                    if q > 0:
                        part = slice(4 * q - 4, 4 * q)
                        dve.wait_ge(S(f"{name}_y"), q)
                        dve.tensor_tensor(res[:, part, :], res[:, part, :], sq2[:, part, :], ALU.add)\
                           .then_inc(S(done), 1)

            def from_psum(name, dst):
                for g in range(1, 8, 2):
                    dve.wait_ge(S(f"{name}_t"), g + 1)
                    dve.tensor_copy(dst[:, 2 * g:2 * g + 2, :], ps[:, g, :].rearrange("p (a t) -> p a t", a=2))\
                       .then_inc(S(f"{name}_fd"), 1)

            link = S("dve_link")
            links = [0]

            def then(ins):
                links[0] += 1
                ins.then_inc(link, 1)
                dve.wait_ge(link, links[0])

            dve.wait_ge(S("const_in"), 32)
            from_psum("x", res)
            norm("attn", res, sq, lambda f: col("attn_g", f), None, a_hi, a_lo)
            lo(0, 0)
            dve.wait_ge(S("csil"), 1)
            clear_mods(0)
            conv = S("conv_tap")

            def conv_read(i, k, bank):
                u, y = ps[:, bank:bank + 1, 0:T], tile(pr, i, k)

                def w(tap):
                    a = COLS["conv"][0] + 16 * tap + k
                    return cols[:, a:a + 1] if isinstance(i, int) else cols[:, bass.ds(i * 2 + a, 1)]
                dve.tensor_scalar(y, u, w(3), None, ALU.mult).then_inc(conv, 1)
                for n in range(1, 4):
                    dve.wait_ge(conv, i * 6 + (3 * k + n))
                    ins = dve.scalar_tensor_tensor(out=y[:, :, n:T], in0=u[:, :, 0:T - n], scalar=w(3 - n),
                                                   in1=y[:, :, n:T], op0=ALU.mult, op1=ALU.add)
                    if n < 3:
                        ins.then_inc(conv, 1)
                ins.then_inc(dve_read, 1)

            reading("conv", conv_read, first=2)

            def copy_read(dst, k0=0):
                def read(i, k, bank):
                    dve.tensor_copy(tile(dst, i, k + k0), psum_tile(bank)).then_inc(dve_read, 1)
                return read

            reading("rest", copy_read(pr, 16))

            dve.memset(g_keep[:, :, :], 1.0).then_inc(S("g_v"), 1)
            dve.memset(g_q[:, :, :], 0.0)
            dve.memset(g_k[:, :, :], 0.0)
            dve.wait_ge(S("g_v"), 1)
            dve.memset(g_keep[:, :, 0:T:CHUNK], 0.0).then_inc(S("g_v"), 1)
            for kv in range(2):
                src_t, pos = ((NKC, "k_pos"), (NVC, "v_pos"))[kv]
                for g in range(2):
                    base = pr[:, src_t + g, :]
                    for part in range(2):
                        v = base[:, 16 * part:16 * part + 16 * N_CMP].rearrange("p (n j) -> p j n", j=16)
                        dst = n_x[:, kv, 16 * part:16 * part + 16, g * N_CMP:(g + 1) * N_CMP]
                        ins = dve.tensor_tensor(dst, v, vbc(col(pos, 16 * part, 16), N_CMP), ALU.add)
                ins.then_inc(S("n_xr"), 1)
            dve.wait_ge(S("g_soft"), 1)
            for h in range(4):
                ins = dve.tensor_scalar(g_kd[:, h, :], ps[:, 2 + h // 2, (h % 2) * T:(h % 2 + 1) * T],
                                        col("gate_b", h), 0.0, ALU.add, ALU.min)
            ins.then_inc(S("g_v"), 1)
            dve.wait_ge(S("g_v"), 3)
            dve.wait_ge(S("g_soft"), 3)
            dve.tensor_tensor(g_kd[:, :, :], g_kd[:, :, :], g_d[:, :, :], ALU.subtract).then_inc(S("g_v"), 1)
            dve.wait_ge(S("g_v"), 4)
            flat = "p a t -> p (a t)"
            dve.tensor_tensor_scan(g_b[:, :, :].rearrange(flat), g_keep[:, :, :].rearrange(flat),
                                   g_kd[:, :, :].rearrange(flat), 0.0, ALU.mult, ALU.add).then_inc(S("g_v"), 1)
            dve.wait_ge(S("g_v"), 5)

            def level_views(t, half):
                v = t.rearrange("p a t -> p (a t)").rearrange("p (n w) -> p n w", w=2 * half)
                return v[:, :, 0:half], v[:, :, half:2 * half]

            def level_diff(lv):
                half = 1 << lv
                b_first, b_second = level_views(g_b[:, :, :], half)
                d_first, d_second = level_views(g_d[:, :, :], half)
                mid = b_first[:, :, half - 1:half].to_broadcast([P, 4 * T // (2 * half), half])
                dve.tensor_tensor(d_first, mid, b_first, ALU.subtract).then_inc(S("g_diff"), 1)
                dve.tensor_tensor(d_second, b_second, mid, ALU.subtract).then_inc(S("g_diff"), 1)

            def level_mul(lv):
                half = 1 << lv
                dve.wait_ge(S("g_dec"), lv + 1)
                dve.wait_ge(S("g_s"), lv + 1)
                k1, _ = level_views(pr[:, KT:KT + 4, :], half)
                _, q2 = level_views(pr[:, QT:QT + 4, :], half)
                d1, d2 = level_views(g_d[:, :, :], half)
                dve.tensor_tensor(level_views(g_k[:, :, :], half)[0], k1, d1, ALU.mult).then_inc(S("g_mul"), 1)
                dve.tensor_tensor(level_views(g_q[:, :, :], half)[1], q2, d2, ALU.mult).then_inc(S("g_mul"), 1)
                dve.wait_ge(S("g_mul"), 2 * (lv + 1))

            def level_mask(n, m):
                dve.wait_ge(S("g_s"), n)
                dst = g_sc if n == 1 else g_tmp
                for tt in range(TT):
                    if n > 2:
                        dve.wait_ge(S("g_add"), 2 * (n - 2) - 1 + tt)
                    dve.tensor_tensor(dst[:, tt, :, :], ps[:, 4 + tt, :].rearrange("p (h t) -> p h t", h=4),
                                      cbc(table[:, m * P:(m + 1) * P], 4), ALU.mult).then_inc(S("g_msk"), 1)
                if n > 1:
                    for tt in range(TT):
                        dve.wait_ge(S("g_msk"), 2 * (n - 1) + tt + 1)
                        dve.tensor_tensor(g_sc[:, tt, :, :], g_sc[:, tt, :, :], g_tmp[:, tt, :, :], ALU.add)\
                           .then_inc(S("g_add"), 1)

            level_diff(0)
            level_mask(1, 6)
            for lv in range(LEVELS):
                level_mul(lv)
                if lv + 1 < LEVELS:
                    level_diff(lv + 1)
                else:
                    last = g_b[:, :, :].rearrange(flat).rearrange("p (n w) -> p n w", w=CHUNK)
                    dve.tensor_tensor(g_d[:, :, :].rearrange(flat).rearrange("p (n w) -> p n w", w=CHUNK),
                                      last[:, :, CHUNK - 1:CHUNK].to_broadcast([P, 16, CHUNK]), last, ALU.subtract)\
                       .then_inc(S("g_diff"), 1)
                level_mask(lv + 2, lv)
            dve.wait_ge(S("g_dec"), LEVELS + 1)
            dve.tensor_tensor(g_kd[:, :, :], pr[:, KT:KT + 4, :], g_d[:, :, :], ALU.mult).then_inc(S("g_kdr"), 1)
            dve.wait_ge(S("g_dec"), LEVELS + 2)
            dve.tensor_tensor(g_qe[:, :, :], pr[:, QT:QT + 4, :], g_d[:, :, :], ALU.mult)
            dve.wait_ge(S("g_kv"), 1)
            dve.wait_ge(S("g_dec"), LEVELS + 3)
            for c in range(3):
                bank = 2 * (c % 2)
                src = ps[:, bank:bank + 2, :].rearrange("p a n -> p (a n)")
                dve.wait_ge(S("g_kv"), c + 1)
                if c == 0:
                    ins = dve.tensor_copy(state[:, 0, :], src)
                else:
                    dve.wait_ge(S("g_state"), c)
                    for h in range(4):
                        part = slice(h * 256, (h + 1) * 256)
                        ins = dve.scalar_tensor_tensor(out=state[:, c, part], in0=state[:, c - 1, part],
                                                       scalar=g_el[:, h, c:c + 1], in1=src[:, part],
                                                       op0=ALU.mult, op1=ALU.add)
                ins.then_inc(S("g_state"), 1)
            dve.wait_ge(S("g_ms"), 1)
            dve.tensor_scalar(g_rs[:, :, :].rearrange(flat), ps[:, 4:6, :].rearrange("p a n -> p (a n)"),
                              1.0 / GLA_DV, EPS * DH, ALU.mult, ALU.add).then_inc(S("g_rsr"), 1)
            dve.wait_ge(S("g_rsr"), 2)
            dve.reciprocal(g_rs[:, :, :], g_rs[:, :, :]).then_inc(S("g_rsr"), 1)
            dve.wait_ge(S("g_rsr"), 3)
            for h in range(4):
                for e in range(2):
                    dve.scalar_tensor_tensor(out=g_y[:, 2 * h + e, :], in0=ps[:, O_BANKS[h], e * T:(e + 1) * T],
                                             scalar=col("gla_g", e), in1=g_rs[:, h, :], op0=ALU.mult, op1=ALU.mult)\
                       .then_inc(S("g_yr"), 1)
            dve.wait_ge(S("g_yr"), 8)
            dve.wait_ge(S("g_silu"), 2)
            dve.tensor_tensor(g_y[:, :, :], g_y[:, :, :], pr[:, GOUT:GOUT + 8, :], ALU.mult).then_inc(S("g_yr"), 1)
            dve.wait_ge(S("g_hi"), 1)
            dve.wait_ge(S("g_yr"), 9)
            dve.tensor_tensor(b_lo[:, 0:8, :], g_y[:, :, :], b_hi[:, 0:8, :].bitcast(F32), ALU.subtract)\
               .then_inc(S("g_out"), 1)
            dve.wait_ge(S("g_out"), 1)

            for n, g in enumerate(("ks_g", "kw_g")):
                dve.tensor_tensor(kq_g[:, n:n + 1], col(g), col("q_g"), ALU.mult).then_inc(S("n_kg"), 1)

            def query_scale(name, bank):
                dve.tensor_scalar(q_rs[:, :, :].rearrange(flat), ps[:, bank, 0:16], 1.0 / DH, EPS, ALU.mult, ALU.add)

            def query_scale_end():
                then(dve.reciprocal(q_rs[:, :, :], q_rs[:, :, :]))
                then(dve.tensor_scalar(q_rs[:, :, :], q_rs[:, :, :], SCALE, None, ALU.mult))
                then(dve.tensor_scalar(q_nrs[:, :, :], q_rs[:, :, :], -1.0, None, ALU.mult))

            dve.wait_ge(S("n_ms"), 1)
            query_scale("n", 5)
            dve.tensor_scalar(n_rs[:, :, :].rearrange(flat), ps[:, 0:2, :].rearrange("p a n -> p (a n)"),
                              1.0 / DH, EPS, ALU.mult, ALU.add).then_inc(S("n_msr"), 1)
            dve.wait_ge(S("n_rt"), 1)
            query_scale_end()
            then(dve.reciprocal(n_rs[:, :, :], n_rs[:, :, :]))
            dve.wait_ge(S("n_kg"), 2)
            for n, t0 in enumerate((NKS, NKW)):
                dve.scalar_tensor_tensor(out=pr[:, t0:t0 + 2, :], in0=pr[:, t0:t0 + 2, :], scalar=kq_g[:, n:n + 1],
                                         in1=n_rs[:, 2 * n:2 * n + 2, :], op0=ALU.mult, op1=ALU.mult)\
                   .then_inc(S("n_qk"), 1)
            dve.wait_ge(S("n_vc"), 1)
            dve.tensor_copy(v_cmp[:, :, :], ps[0:N_CMP, 4, 0:2 * P].rearrange("p (a n) -> p a n", a=2))
            dve.wait_ge(S("n_cms"), 1)
            dve.tensor_scalar(c_rs[:, :], ps[:, 2, 0:2 * N_CMP], 1.0 / DH, EPS, ALU.mult, ALU.add)\
               .then_inc(S("n_crs"), 1)
            dve.wait_ge(S("n_crt"), 1)
            dve.reciprocal(c_rs[:, :], c_rs[:, :]).then_inc(S("n_crs"), 1)
            dve.wait_ge(S("n_crs"), 2)
            dve.scalar_tensor_tensor(out=k_cmp[:, :], in0=ps[:, 6, 0:2 * N_CMP], scalar=col("kc_g"),
                                     in1=c_rs[:, :], op0=ALU.mult, op1=ALU.mult).then_inc(S("n_kcg"), 1)
            dve.wait_ge(S("n_kcg"), 1)
            dve.tensor_scalar(k_cmp[:, :], k_cmp[:, :], col("q_g"), None, ALU.mult).then_inc(S("n_kcn"), 1)
            dve.wait_ge(S("n_cs"), 1)
            dve.wait_ge(S("n_gs"), 1)
            add_a, ok_a = CONS["cmp_add"][0], CONS["cmp_ok"][0]
            for tt in range(TT):
                cs, mx, den = c_s[:, tt, :, :], c_mx[:, tt, :], c_den[:, tt, :]
                sc = ps[:, 2 + tt, 0:P].rearrange("p (h n) -> p h n", h=8)[:, :, 0:N_CMP]
                add = cons[:, add_a + tt * N_CMP:add_a + (tt + 1) * N_CMP]
                then(dve.tensor_tensor(cs, sc, vbc(q_rs[:, tt, :], N_CMP), ALU.mult))
                then(dve.tensor_tensor(cs, cs, cbc(add, 8), ALU.add))
                then(dve.tensor_reduce(mx, cs, AX.X, ALU.max))
                dve.tensor_tensor(cs, cs, vbc(mx, N_CMP), ALU.subtract).then_inc(S("c_sub"), 1)
            for tt in range(TT):
                cs, mx, den = c_s[:, tt, :, :], c_mx[:, tt, :], c_den[:, tt, :]
                ok = cons[:, ok_a + tt * N_CMP:ok_a + (tt + 1) * N_CMP]
                dve.wait_ge(S("c_exp"), tt + 1)
                then(dve.tensor_reduce(den, cs, AX.X, ALU.add))
                then(dve.reciprocal(den, den))
                then(dve.tensor_tensor(den, den, gates[:, tt, 0:24:3], ALU.mult))
                then(dve.tensor_tensor(cs, cs, cbc(ok, 8), ALU.mult))
                dve.tensor_tensor(c_p[:, tt, :, :], cs, vbc(den, N_CMP), ALU.mult).then_inc(S("c_ready"), 1)

            def attend(name):
                a = att(name)
                base, tt, kind = a["base"], a["tt"], a["kind"]
                for h in range(8):
                    bank = 2 + h % 3
                    dve.wait_ge(S("at_sc"), base + h + 1)
                    for part, b, m in a["mask"]:
                        blk = ps[:, bank, part * T + b * P:part * T + (b + 1) * P]
                        last = dve.tensor_tensor(blk, blk, con(m), ALU.add)
                    if a["mask"]:
                        then(last)
                    if kind == "n":
                        src = ps[:, bank, :].rearrange("p (a n) -> p a n", a=2)[:, :, 0:a["keys"]]
                        mx, nb = at_max[:, 2 * h:2 * h + 2], at_nb[:, 2 * h:2 * h + 2]
                    else:
                        src, mx, nb = ps[:, bank, :], at_max[:, h:h + 1], at_nb[:, h:h + 1]
                    then(dve.tensor_reduce(mx, src, AX.X, ALU.max))
                    if kind == "b":
                        ins = dve.tensor_scalar(nb, mx, -SCALE, neg_sink[:, h:h + 1], ALU.mult, ALU.min)
                    else:
                        ins = dve.tensor_scalar(nb, mx, q_nrs[:, tt, h:h + 1], None, ALU.mult)
                    ins.then_inc(S("at_nb_r"), 1)
                n = 16 if kind == "n" else 8
                if kind == "b":
                    dve.wait_ge(S("at_nb_r"), base + 8)
                    dve.tensor_tensor(at_sink[:, :], at_nb[:, 0:8], col("sink", 0, 8), ALU.add).then_inc(S("at_sd"), 1)
                dve.wait_ge(S("at_exp"), base + 8)
                if kind == "b":
                    dve.wait_ge(S("at_se"), tt + 1)
                    then(dve.tensor_tensor(at_den[:, 0:8], at_den[:, 0:8], at_sink[:, :], ALU.add))
                then(dve.reciprocal(at_coef[:, 0:n], at_den[:, 0:n]))
                if kind == "n":
                    g = gates[:, tt, :].rearrange("p (h c) -> p h c", c=3)[:, :, 1:3]
                    then(dve.tensor_tensor(at_coef[:, :].rearrange("p (h c) -> p h c", c=2),
                                           at_coef[:, :].rearrange("p (h c) -> p h c", c=2), g, ALU.mult))

                def scale(h):
                    if kind == "n":
                        for part in range(2):
                            p_ap = a["prob"][:, h, part, 0:a["keys"]]
                            ins = dve.tensor_scalar(p_ap, p_ap, at_coef[:, 2 * h + part:2 * h + part + 1], None, ALU.mult)
                    else:
                        p_ap = a["prob"][:, h, :, :]
                        ins = dve.tensor_scalar(p_ap, p_ap, at_coef[:, h:h + 1], None, ALU.mult)
                    ins.then_inc(S("at_scl"), 1)

                def read(h):
                    dve.wait_ge(S("at_pv"), base + h + 1)
                    dve.tensor_copy(pr[:, a["q"](h), a["cols"]], ps[:, 5 + h % 2, 0:P]).then_inc(S("at_out"), 1)

                scale(0)
                scale(1)
                for h in range(8):
                    if h + 2 < 8:
                        scale(h + 2)
                    read(h)

            attend("n0")
            attend("n1")
            dve.wait_ge(S("mix_hi"), 1)
            dve.wait_ge(S("at_out"), 16)
            dve.tensor_tensor(b_lo[:, 8:16, :], pr[:, NQ:NQ + 8, :], b_hi[:, 8:16, :].bitcast(F32), ALU.subtract)\
               .then_inc(S("mix_lo"), 1)

            def add_res(i, k, bank):
                dve.tensor_tensor(tile(res, i, k), psum_tile(bank), tile(res, i, k), ALU.add).then_inc(dve_read, 1)

            reading("out", add_res)

            norm("ffn", res, sq, lambda f: col("ffn_g", f), None, a_hi, a_lo)
            dve.memset(gated[:, 0, :], 0.0).then_inc(S("gate_y"), 1)
            gate_hi = S("gate_hi")

            def split_out(i, per, n, other, dst_k):
                y = gated[:, dst_k % per:dst_k % per + 1, :]
                dve.wait_ge(silu_ready, i * per + (n + 2))
                dve.tensor_tensor(y, other, sg[:, 0:1, :], ALU.mult).then_inc(S("gate_y"), 1)
                dve.wait_ge(S("gate_y"), i * per + (n + 2))
                bh = b_hi[:, dst_k:dst_k + 1, :] if isinstance(i, int) else b_hi[:, bass.ds(i * per + dst_k, 1), :]
                bl = b_lo[:, dst_k:dst_k + 1, :] if isinstance(i, int) else b_lo[:, bass.ds(i * per + dst_k, 1), :]
                dve.tensor_copy(bh, y).then_inc(gate_hi, 1)
                dve.wait_ge(gate_hi, i * per + (n + 1))
                dve.tensor_tensor(bl, y, bh.bitcast(F32), ALU.subtract).then_inc(S("gate_lo"), 1)

            for c, n in enumerate(CHUNKS):
                done = sum(CHUNKS[:c])

                def up_read(i, k, bank, done=done):
                    if k % 2:
                        split_out(i, 1, done + k // 2, psum_tile(bank), k // 2)
                reading(f"up{c}", up_read)
                reading(f"down{c}", add_res)

            dve.wait_ge(S("mods_read"), 6)
            for c in range(2):
                dve.scalar_tensor_tensor(out=ev_gain[:, :, c], in0=mods[:, 16:32, c], scalar=1.0,
                                         in1=col("ev_pre", 0, 16), op0=ALU.add, op1=ALU.mult)
            dve.tensor_tensor(ev_gate[:, :], mods[:, 32:48, 0], col("ev_post", 0, 16), ALU.mult)
            dve.tensor_scalar(neg_sink[:, :], col("sink", 0, 8), -1.0, None, ALU.mult)
            then(dve.tensor_scalar(rot_g[:, 0, :], con("rot"), col("ev_qn"), None, ALU.mult))

            norm("ev", res, sq, lambda f: ev_gain[:, f, 0:1], lambda f: mods[:, f, 0:1], a_hi, a_lo)
            dve.wait_ge(S("ev_lo"), 16)
            from_psum("ctx", ctx_f)
            norm("ctx", ctx_f, sq2, lambda f: ev_gain[:, f, 1:2], lambda f: mods[:, f, 1:2], b_hi, b_lo)

            def kv_read(i, k, bank):
                dve.tensor_copy(tile(pr, i, k), psum_tile(bank))
                dve.tensor_copy(tile(pr, i, k + 8), psum_tile(2 + bank)).then_inc(dve_read, 1)

            reading("ev_kv", kv_read)
            reading("ev_q", copy_read(pr, 16))
            dve.wait_ge(S("e_ms"), 1)
            query_scale("e", 6)
            dve.tensor_scalar(e_rs[:, :, :].rearrange(flat), ps[:, 2:4, :].rearrange("p a n -> p (a n)"),
                              1.0 / DH, EPS, ALU.mult, ALU.add).then_inc(S("e_msr"), 1)
            dve.wait_ge(S("e_rt"), 1)
            query_scale_end()
            then(dve.reciprocal(e_rs[:, :, :], e_rs[:, :, :]))
            for t0, n, r0, g in ((0, 2, 0, "ev_kn"), (8, 2, 2, "ev_kn")):
                dve.scalar_tensor_tensor(out=pr[:, t0:t0 + n, :], in0=pr[:, t0:t0 + n, :], scalar=col(g),
                                         in1=e_rs[:, r0:r0 + n, :], op0=ALU.mult, op1=ALU.mult)\
                   .then_inc(S("e_nrm"), 1)
            dve.wait_ge(S("e_nrm"), 2)
            for n, t0 in enumerate(ROPE_PAIRS):
                pair, tmp = pr[:, t0:t0 + 2, :], e_rot[:, n % 2, :, :]
                dve.wait_ge(S("e_rp"), n + 1)
                dve.tensor_tensor(tmp, ps[:, ROPE_BANKS[n % 3], :].rearrange("p (a t) -> p a t", a=2), cbc(con("sin"), 2),
                                  ALU.mult).then_inc(S("e_rot"), 1)
                if 16 <= t0 < 24:
                    then(dve.scalar_tensor_tensor(out=pair, in0=pair, scalar=col("ev_qn"), in1=cbc(con("cos"), 2),
                                                  op0=ALU.mult, op1=ALU.mult))
                else:
                    then(dve.tensor_tensor(pair, pair, cbc(con("cos"), 2), ALU.mult))
                dve.tensor_tensor(pair, pair, tmp, ALU.add).then_inc(S("e_rope"), 1)
                dve.wait_ge(S("e_rope"), n + 1)
            for name in ("a0", "a1", "b0", "b1"):
                attend(name)
            dve.wait_ge(S("at_out"), 48)

            def z_read(done, k0):
                def read(i, k, bank):
                    other = tile(pr, i, k + k0)
                    split_out(i, 2, FFN_TILES + done + k, other, k)
                return read

            reading("ev_z", z_read(0, 16))
            reading("ev_out", copy_read(pr))
            post_norm("ev_post", ev_gate, "ev_res")
            dve.wait_ge(S("ev_res"), 4)

            dve.wait_ge(S("mods_read"), len(MOD_STAGES))
            dve.scalar_tensor_tensor(out=od_gain[:, :], in0=mods[:, 64:80, 0], scalar=1.0,
                                     in1=col("od_pre", 0, 16), op0=ALU.add, op1=ALU.mult)
            then(dve.tensor_tensor(od_gate[:, :], mods[:, 80:96, 0], col("od_post", 0, 16), ALU.mult))
            norm("od", res, sq, lambda f: od_gain[:, f:f + 1], lambda f: mods[:, 48 + f, 0:1], a_hi, a_lo)
            W = T + 8

            def pool(g):
                dve.wait_ge(dve_read, dve_reads("od_u") + 4 * (g + 1))
                u = pr[:, 4 * g:4 * g + 4, :]
                a_buf, b_buf = f_a, f_b
                dve.memset(a_buf[:, :, T:W], 0.0)
                then(dve.tensor_copy(a_buf[:, :, 0:T], u))
                for lv in range(g + 1):
                    w = 1 << lv
                    dve.tensor_copy(b_buf[:, :, 0:w], a_buf[:, :, 0:w])
                    then(dve.tensor_tensor(b_buf[:, :, w:W], a_buf[:, :, w:W], a_buf[:, :, 0:W - w], ALU.add))
                    a_buf, b_buf = b_buf, a_buf
                lag = (1 << g) - 1
                y = pooled[:, 4 * g:4 * g + 4, :]
                then(dve.tensor_tensor(y, a_buf[:, :, lag:lag + T], cbc(table[:, g * T:(g + 1) * T], 4), ALU.mult))
                dve.tensor_tensor(y, y, u, ALU.subtract).then_inc(S("pool_y"), 1)

            def pool_rest(g):
                dve.wait_ge(S("pool_hi"), g + 1)
                dve.tensor_tensor(b_lo[:, 4 * g:4 * g + 4, :], pooled[:, 4 * g:4 * g + 4, :],
                                  b_hi[:, 4 * g:4 * g + 4, :].bitcast(F32), ALU.subtract).then_inc(S("pool_lo"), 1)

            dve.wait_ge(S("counts_in"), 16)
            reading("od_u", copy_read(pr), splits=(4, 8, 12), between=lambda k: pool(k // 4 - 1))
            for g in range(3):
                pool_rest(g)
            pool(3)
            pool_rest(3)
            for g in range(4):
                s = FIRST["pool"] + g
                lo(0, s + 1)
                dve.wait_ge(halves_used, 2 * s + 2)
                for n in range(4):
                    ins = dve.tensor_scalar(pr[:, 4 * g + n, :], ps[:, 2 * (s % 2) + n // 2, (n % 2) * T:(n % 2 + 1) * T],
                                            col("pool_s", 4 * g + n), None, ALU.mult)
                ins.then_inc(dve_read, 1)
            dve.wait_ge(dve_read, dve_reads("od_z"))
            reading("od_z", z_read(16, 0))
            reading("od_out", copy_read(pr))
            post_norm("od_post", od_gate, "final")
            for g in range(4):
                dve.wait_ge(S("o_t"), 2 * g + 2)
                dve.tensor_copy(o_tok[:, 1, g * 512:(g + 1) * 512], ps[:, 4 + g, :]).then_inc(S("o_tok1"), 1)


def _tiles(w):
    k, n = w.shape
    kp = -(-k // 1024) * 1024
    if kp != k:
        w = np.concatenate([w, np.zeros((kp - k, n), w.dtype)])
    w = w.reshape(kp // 1024, 8, P, n // P, P)
    return w.transpose(3, 0, 2, 1, 4).reshape(-1, P, HALF)


def _column(v):
    v = np.asarray(v).reshape(-1)
    return v.reshape(-1, P).T


def _shape_constants():
    t = np.arange(T)
    ident = np.eye(P, dtype=np.float32)
    i, j = np.arange(P)[:, None], np.arange(P)[None, :]
    above = np.where(j > i, NEG, 0.0)
    below = np.where(j < i, NEG, 0.0)
    rot = np.zeros((P, P))
    rot[np.arange(64) + 64, np.arange(64)] = -1.0
    rot[np.arange(64), np.arange(64) + 64] = 1.0
    inv = (np.float32(10000.0) ** (-np.arange(32, dtype=np.float32) / np.float32(32))).astype(np.float32)
    row, colm = (t // 64).astype(np.float32), (t % 64).astype(np.float32)
    ang = np.concatenate([row[:, None] * inv, colm[:, None] * inv], axis=-1).astype(np.float32)
    cos, sin = np.cos(ang).T, np.sin(ang).T
    cos, sin = np.concatenate([cos, cos]), np.concatenate([sin, sin])
    end = np.arange(N_CMP) * CMP_STRIDE + CMP_W - 1
    ok = (end[None, :] <= t[:, None]).reshape(TT, P, N_CMP).transpose(1, 0, 2).reshape(P, -1)
    cons = np.concatenate([ident, np.ones((P, P)), above, below, rot, cos, sin,
                           np.where(ok, 0.0, NEG), ok.astype(np.float32)], axis=1).astype(np.float32)
    masks = []
    for lv in range(LEVELS):
        h = 1 << lv
        masks.append((i // (2 * h) == j // (2 * h)) & (i % (2 * h) < h) & (j % (2 * h) >= h))
    masks.append(i == j)
    masks = np.concatenate(masks, axis=1).astype(np.float32)
    counts = []
    for w in (2, 4, 8, 16):
        n = np.clip(t + w // 2, 0, T) - np.clip(t - w // 2, 0, T)
        counts.append(np.broadcast_to((1.0 / n).astype(np.float32), (P, T)))
    return cons, masks, np.concatenate(counts, axis=1)


def _pack(a):
    w = np.asarray(a["w_in"])[0]
    gla = w[:, 0:2048]
    lr = w[:, 2048:2064]
    gout = w[:, 2064:3088]
    nq = w[:, 3088:4112]
    kc, vc, ks, vs, kw, vw = (w[:, 4112 + 256 * n:4112 + 256 * (n + 1)] for n in range(6))
    ng = w[:, 5648:5672]
    z = np.zeros
    last = np.concatenate([lr, z((D, GATE_ROW - 16), w.dtype), ng, z((D, P - GATE_ROW - 24), w.dtype)], axis=1)
    parts = [_tiles(np.concatenate([gla, gout, nq, ks, kw, kc, vc, vs, vw, last], axis=1)),
             _tiles(np.asarray(a["w_out"])[0])]
    wg, wu, wd = (np.asarray(a[n])[0] for n in ("w_gate", "w_up", "w_down"))
    at = 0
    for n in CHUNKS:
        f = slice(at * P, (at + n) * P)
        g, u = _tiles(wg[:, f]), _tiles(wu[:, f])
        parts.append(np.stack([g.reshape(n, 2, P, HALF), u.reshape(n, 2, P, HALF)], axis=1).reshape(-1, P, HALF))
        parts.append(_tiles(wd[f]))
        at += n
    ev = np.asarray(a["ev_w_in_2"])[0]
    parts += [_tiles(ev[:, 2048:3072]), _tiles(ev[:, 0:2048]), _tiles(ev[:, 3072:]), _tiles(np.asarray(a["ev_w_out_2"])[0])]
    od = np.asarray(a["od_w_in_2"])[0]
    pool = np.asarray(a["od_pool_w_2"])[0].reshape(4, 4, P, 2, 2, P)
    parts += [_tiles(od[:, 0:2048]), pool.transpose(0, 3, 2, 4, 1, 5).reshape(-1, P, HALF),
              _tiles(od[:, 2048:]), _tiles(np.asarray(a["od_w_out_2"])[0])]
    w_main = np.concatenate(parts)
    assert w_main.shape[0] == HALVES
    mod = [np.asarray(a[n])[0].reshape(DT, P, 6, HALF).transpose(2, 0, 1, 3) for n in ("ev_mod_w_2", "od_mod_w_2")]
    groups = np.concatenate(mod)[[MOD_GROUPS[n] for n in MOD_STAGES]].reshape(-1, P, HALF)
    w_side = np.concatenate([groups[:CMP_AT], _tiles(np.asarray(a["cmp_k_w1"])[0]),
                             _tiles(np.asarray(a["cmp_v_w1"])[0]), groups[CMP_AT:]])
    assert w_side.shape[0] == SIDE_HALVES
    cvec = np.stack([_column(a["c_2"]), _column(a["c_ctx_2"])], axis=2).reshape(P, 32)
    vectors = {
        "attn_g": _column(a["attn_norm_g"]), "conv": _column(a["gla_conv_w"]), "gate_b": _column(a["gla_gate_b"]),
        "gla_g": _column(a["gla_norm_g"]), "q_g": _column(a["nsa_q_norm_g"]), "kc_g": _column(a["nsa_kc_norm_g"]),
        "ks_g": _column(a["nsa_ks_norm_g"]), "kw_g": _column(a["nsa_kw_norm_g"]), "k_pos": _column(a["cmp_k_pos"]),
        "v_pos": _column(a["cmp_v_pos"]), "ffn_g": _column(a["ffn_norm_g"]), "ev_pre": _column(a["ev_pre_g_2"]),
        "ev_post": _column(a["ev_post_g_2"]), "od_pre": _column(a["od_pre_g_2"]), "od_post": _column(a["od_post_g_2"]),
        "pool_s": _column(a["od_pool_scale_2"]),
        "mod_b": np.concatenate([_column(a["ev_mod_b_2"]), _column(a["od_mod_b_2"])], axis=1),
        "cvec": cvec, "ev_qn": _column(a["ev_q_norm_2"]), "ev_kn": _column(a["ev_k_norm_2"]),
        "sink": np.broadcast_to(np.asarray(a["ev_sink_2"]).reshape(1, 8), (P, 8)),
    }
    cols = np.concatenate([vectors[n] for n in COLS], axis=1)
    assert cols.shape == (P, NCOLS)
    cons, masks, counts = _shape_constants()
    cmp_w2 = np.stack([np.asarray(a["cmp_k_w2"])[0], np.asarray(a["cmp_v_w2"])[0]], axis=1)
    return {
        "x_in": np.asarray(a["x"])[0], "ctx_tok": np.asarray(a["ctx_2"])[0], "w_main": w_main, "w_side": w_side,
        "cols_in": cols, "cons_in": cons, "masks_in": masks, "counts_tab": counts,
        "gate_w2_in": np.asarray(a["gla_gate_w2"])[0], "cmp_w2_in": cmp_w2,
    }


def kernel(**inputs):
    import concourse.bacc as _bacc
    from concourse.bass_utils import run_bass_kernel_spmd as _run

    nc = _bacc.Bacc("TRN2", target_bir_lowering=False, num_devices=1)
    arrays = {name: np.ascontiguousarray(a) for name, a in _pack(inputs).items()}
    args = [nc.dram_tensor(name, a.shape, mybir.dt.from_np(a.dtype), kind="ExternalInput").ap()
            for name, a in arrays.items()]
    args.append(nc.dram_tensor("y_out", (T, D), F32, kind="ExternalOutput").ap())
    build(nc, *args)
    r = _run(nc, [arrays], core_ids=[0])
    return r.results[0]["y_out"].reshape(1, T, D)
```
